# Optimizing a Trainium2 kernel written in Bass

```python
import math
import jax, jax.numpy as jnp
from jax import lax
import numpy as np

D_MODEL = 2048
BATCH = 1
SEQ = 256
DEPTH = 2

CHUNK = 64
N_A = max(1, DEPTH // 2)
N_B = DEPTH - N_A
EPS = 1e-6
PLE_DIM = 256
D_FF = 4 * D_MODEL

SSM_EXPAND = 2
D_INNER = SSM_EXPAND * D_MODEL
SSM_HEADDIM = 64
SSM_HEADS = D_INNER // SSM_HEADDIM
SSM_GROUPS = 8
SSM_STATE = 128
CONV_W = 4
GN = SSM_GROUPS * SSM_STATE
CONV_DIM = D_INNER + 2 * GN
IN_PROJ_DIM = D_INNER + CONV_DIM + SSM_HEADS

MLA_HEADS = 16
QK_NOPE = 128
QK_ROPE = 64
QK_HEAD = QK_NOPE + QK_ROPE
V_HEAD = 128
Q_LORA = 512
KV_LORA = 512
ROPE_THETA = 10000.0
Q_BLOCK = 128

kernel_name = 'yoco_mamba2_mla_hybrid'

def rmsnorm(x, g):
    xf = x.astype(jnp.float32)
    y = xf * lax.rsqrt(jnp.mean(xf * xf, axis=-1, keepdims=True) + EPS)
    return (y * g.astype(jnp.float32)).astype(x.dtype)

def rope(x, positions):
    half = x.shape[-1] // 2
    freqs = ROPE_THETA ** (-jnp.arange(half, dtype=jnp.float32) / half)
    ang = positions.astype(jnp.float32)[..., None] * freqs
    ang = ang.reshape(ang.shape[:2] + (1,) * (x.ndim - 3) + (half,))
    cos, sin = jnp.cos(ang), jnp.sin(ang)
    xf = x.astype(jnp.float32)
    x1, x2 = xf[..., :half], xf[..., half:]
    return jnp.concatenate([x1 * cos - x2 * sin, x2 * cos + x1 * sin], axis=-1).astype(x.dtype)

def causal_depthwise_conv(u, w, b):
    out = lax.conv_general_dilated(
        u, w[:, None, :].astype(u.dtype), window_strides=(1,), padding=[(CONV_W - 1, 0)],
        dimension_numbers=('NWC', 'WIO', 'NWC'), feature_group_count=u.shape[-1])
    return out + b.astype(u.dtype)

def ssd_chunked_scan(x, a, bm, cm):
    bsz, s, h, p = x.shape
    g, n = bm.shape[-2:]
    hg = h // g
    nc = s // CHUNK
    x = x.reshape(bsz, nc, CHUNK, g, hg, p)
    a = a.reshape(bsz, nc, CHUNK, g, hg).transpose(0, 1, 3, 4, 2)
    bm = bm.reshape(bsz, nc, CHUNK, g, n)
    cm = cm.reshape(bsz, nc, CHUNK, g, n)
    a_cs = jnp.cumsum(a, axis=-1)
    causal = jnp.tril(jnp.ones((CHUNK, CHUNK), dtype=bool))
    seg = a_cs[..., :, None] - a_cs[..., None, :]
    decay = jnp.exp(jnp.where(causal, seg, -jnp.inf))
    cb = jnp.einsum('bclgn,bcsgn->bcgls', cm, bm)
    y_diag = jnp.einsum('bcgls,bcghls,bcsghp->bclghp', cb, decay, x)
    decay_states = jnp.exp(a_cs[..., -1:] - a_cs)
    states = jnp.einsum('bclgn,bcghl,bclghp->bcghpn', bm, decay_states, x)
    chunk_decay = jnp.exp(a_cs[..., -1])

    def step(carry, inp):
        st, dec = inp
        return carry * dec[..., None, None] + st, carry

    init = jnp.zeros((bsz, g, hg, p, n), dtype=x.dtype)
    _, prev_states = lax.scan(step, init, (jnp.moveaxis(states, 1, 0), jnp.moveaxis(chunk_decay, 1, 0)))
    prev_states = jnp.moveaxis(prev_states, 0, 1)
    y_off = jnp.einsum('bclgn,bcghpn,bcghl->bclghp', cm, prev_states, jnp.exp(a_cs))
    return (y_diag + y_off).reshape(bsz, s, h, p)

def mamba2_mixer(hn, w_in, conv_w, conv_b, dt_bias, a_log, d_skip, norm_g, w_out):
    bsz, s, _ = hn.shape
    zxbcdt = hn @ w_in
    z = zxbcdt[..., :D_INNER]
    xbc = zxbcdt[..., D_INNER:D_INNER + CONV_DIM]
    dt = zxbcdt[..., D_INNER + CONV_DIM:]
    xbc = jax.nn.silu(causal_depthwise_conv(xbc, conv_w, conv_b))
    xs = xbc[..., :D_INNER].reshape(bsz, s, SSM_HEADS, SSM_HEADDIM).astype(jnp.float32)
    bm = xbc[..., D_INNER:D_INNER + GN].reshape(bsz, s, SSM_GROUPS, SSM_STATE).astype(jnp.float32)
    cm = xbc[..., D_INNER + GN:].reshape(bsz, s, SSM_GROUPS, SSM_STATE).astype(jnp.float32)
    dt = jax.nn.softplus(dt.astype(jnp.float32) + dt_bias.astype(jnp.float32))
    a = -jnp.exp(a_log.astype(jnp.float32))
    y = ssd_chunked_scan(xs * dt[..., None], dt * a, bm, cm)
    y = y + d_skip.astype(jnp.float32)[:, None] * xs
    y = y.reshape(bsz, s, D_INNER) * jax.nn.silu(z.astype(jnp.float32))
    y = rmsnorm(y.reshape(bsz, s, SSM_GROUPS, D_INNER // SSM_GROUPS),
                norm_g.reshape(SSM_GROUPS, D_INNER // SSM_GROUPS)).reshape(bsz, s, D_INNER)
    return y.astype(hn.dtype) @ w_out

def mla_shared_kv(h, kv_in_norm, w_dkv, ckv_norm, w_kr, w_uk, w_uv, k_nope_norm, k_rope_norm, positions):
    bsz, s, _ = h.shape
    hn = rmsnorm(h, kv_in_norm)
    c_kv = rmsnorm(hn @ w_dkv, ckv_norm)
    k_rope = rope(rmsnorm(hn @ w_kr, k_rope_norm), positions)
    k_nope = rmsnorm((c_kv @ w_uk).reshape(bsz, s, MLA_HEADS, QK_NOPE), k_nope_norm)
    v = (c_kv @ w_uv).reshape(bsz, s, MLA_HEADS, V_HEAD)
    return k_nope, k_rope, v

def chunk_causal_attention(q_nope, q_rope, k_nope, k_rope, v):
    bsz, s, h, _ = q_nope.shape
    nb = s // Q_BLOCK
    scale = QK_HEAD ** -0.5
    qn = jnp.moveaxis(q_nope.reshape(bsz, nb, Q_BLOCK, h, QK_NOPE), 1, 0)
    qr = jnp.moveaxis(q_rope.reshape(bsz, nb, Q_BLOCK, h, QK_ROPE), 1, 0)
    key_chunk = jnp.arange(s) // CHUNK

    def one_block(args):
        i, qn_b, qr_b = args
        sc = (jnp.einsum('bqhd,bkhd->bhqk', qn_b, k_nope)
              + jnp.einsum('bqhr,bkr->bhqk', qr_b, k_rope)).astype(jnp.float32) * scale
        q_chunk = (i * Q_BLOCK + jnp.arange(Q_BLOCK)) // CHUNK
        mask = key_chunk[None, :] <= q_chunk[:, None]
        probs = jax.nn.softmax(jnp.where(mask, sc, -jnp.inf), axis=-1)
        return jnp.einsum('bhqk,bkhd->bqhd', probs.astype(v.dtype), v)

    out = lax.map(one_block, (jnp.arange(nb), qn, qr))
    return jnp.moveaxis(out, 0, 1).reshape(bsz, s, h * V_HEAD)

def mla_mixer(hn, w_dq, cq_norm, w_uq, q_nope_norm, q_rope_norm, w_o, k_nope, k_rope, v, positions):
    bsz, s, _ = hn.shape
    c_q = rmsnorm(hn @ w_dq, cq_norm)
    q = (c_q @ w_uq).reshape(bsz, s, MLA_HEADS, QK_HEAD)
    q_nope = rmsnorm(q[..., :QK_NOPE], q_nope_norm)
    q_rope = rope(rmsnorm(q[..., QK_NOPE:], q_rope_norm), positions)
    return chunk_causal_attention(q_nope, q_rope, k_nope, k_rope, v) @ w_o

def sq_relu_mlp(hn, w1, w2):
    return jnp.square(jax.nn.relu(hn @ w1)) @ w2

def per_layer_input(h, p_i, g, w_gate, w_proj):
    gate = jax.nn.sigmoid(rmsnorm(h, g) @ w_gate)
    return h + gate * (p_i @ w_proj)

def setup_inputs(seed: int = 0) -> dict:
    key = jax.random.key(seed)
    keys = list(jax.random.split(key, 48))
    f32 = jnp.float32

    def nk():
        return keys.pop()

    def nrm(shape, fan_in, scale=1.0):
        return jax.random.normal(nk(), shape, f32) * (scale * fan_in ** -0.5)

    def gain(shape):
        return 1.0 + 0.05 * jax.random.normal(nk(), shape, f32)

    out_s = (2.0 * DEPTH) ** -0.5
    x = jax.random.normal(nk(), (BATCH, SEQ, D_MODEL), f32)
    p = jax.random.normal(nk(), (DEPTH, BATCH, SEQ, PLE_DIM), f32)
    positions = jnp.tile(jnp.arange(SEQ, dtype=jnp.int32)[None, :], (BATCH, 1))
    dt = jnp.exp(jax.random.uniform(nk(), (N_A, SSM_HEADS), f32, math.log(1e-3), math.log(1e-1)))
    return {
        'x': x,
        'p': p,
        'positions': positions,
        'ln_mix': gain((DEPTH, D_MODEL)),
        'ln_mlp': gain((DEPTH, D_MODEL)),
        'mlp_w1': nrm((DEPTH, D_MODEL, D_FF), D_MODEL),
        'mlp_w2': nrm((DEPTH, D_FF, D_MODEL), D_FF, out_s),
        'ple_norm': gain((DEPTH, D_MODEL)),
        'ple_gate_w': nrm((DEPTH, D_MODEL, D_MODEL), D_MODEL),
        'ple_proj_w': nrm((DEPTH, PLE_DIM, D_MODEL), PLE_DIM, out_s),
        'ssm_in_w': nrm((N_A, D_MODEL, IN_PROJ_DIM), D_MODEL),
        'ssm_conv_w': nrm((N_A, CONV_W, CONV_DIM), CONV_W),
        'ssm_conv_b': 0.02 * jax.random.normal(nk(), (N_A, CONV_DIM), f32),
        'ssm_dt_bias': dt + jnp.log(-jnp.expm1(-dt)),
        'ssm_a_log': jnp.log(jax.random.uniform(nk(), (N_A, SSM_HEADS), f32, 1.0, 16.0)),
        'ssm_d': gain((N_A, SSM_HEADS)),
        'ssm_norm': gain((N_A, D_INNER)),
        'ssm_out_w': nrm((N_A, D_INNER, D_MODEL), D_INNER, out_s),
        'kv_in_norm': gain((D_MODEL,)),
        'w_dkv': nrm((D_MODEL, KV_LORA), D_MODEL),
        'ckv_norm': gain((KV_LORA,)),
        'w_kr': nrm((D_MODEL, QK_ROPE), D_MODEL),
        'w_uk': nrm((KV_LORA, MLA_HEADS * QK_NOPE), KV_LORA),
        'w_uv': nrm((KV_LORA, MLA_HEADS * V_HEAD), KV_LORA),
        'k_nope_norm': gain((QK_NOPE,)),
        'k_rope_norm': gain((QK_ROPE,)),
        'w_dq': nrm((N_B, D_MODEL, Q_LORA), D_MODEL),
        'cq_norm': gain((N_B, Q_LORA)),
        'w_uq': nrm((N_B, Q_LORA, MLA_HEADS * QK_HEAD), Q_LORA),
        'q_nope_norm': gain((N_B, QK_NOPE)),
        'q_rope_norm': gain((N_B, QK_ROPE)),
        'mla_out_w': nrm((N_B, MLA_HEADS * V_HEAD, D_MODEL), MLA_HEADS * V_HEAD, out_s),
    }

def reference(x, p, positions, ln_mix, ln_mlp, mlp_w1, mlp_w2, ple_norm, ple_gate_w, ple_proj_w,
              ssm_in_w, ssm_conv_w, ssm_conv_b, ssm_dt_bias, ssm_a_log, ssm_d, ssm_norm, ssm_out_w,
              kv_in_norm, w_dkv, ckv_norm, w_kr, w_uk, w_uv, k_nope_norm, k_rope_norm,
              w_dq, cq_norm, w_uq, q_nope_norm, q_rope_norm, mla_out_w):
    h = x
    shared = None
    for i in range(DEPTH):
        hn = rmsnorm(h, ln_mix[i])
        if i < N_A:
            j = i
            h = h + mamba2_mixer(hn, ssm_in_w[j], ssm_conv_w[j], ssm_conv_b[j], ssm_dt_bias[j],
                                 ssm_a_log[j], ssm_d[j], ssm_norm[j], ssm_out_w[j])
        else:
            j = i - N_A
            if shared is None:
                shared = mla_shared_kv(h, kv_in_norm, w_dkv, ckv_norm, w_kr, w_uk, w_uv,
                                       k_nope_norm, k_rope_norm, positions)
            k_nope, k_rope, v = shared
            h = h + mla_mixer(hn, w_dq[j], cq_norm[j], w_uq[j], q_nope_norm[j], q_rope_norm[j],
                              mla_out_w[j], k_nope, k_rope, v, positions)
        h = h + sq_relu_mlp(rmsnorm(h, ln_mlp[i]), mlp_w1[i], mlp_w2[i])
        h = per_layer_input(h, p[i], ple_norm[i], ple_gate_w[i], ple_proj_w[i])
    return h


_drawn_inputs = setup_inputs


def setup_inputs(seed=0):
    import zlib

    import numpy as np

    out = dict(_drawn_inputs(seed))
    spreads = {}
    factors = {'ple_norm': 8.0,
     'ssm_conv_b': 4.566,
     'ssm_d': 3.398,
     'kv_in_norm': 8.0,
     'ckv_norm': 8.0,
     'k_nope_norm': 8.0,
     'k_rope_norm': 8.0,
     'cq_norm': 8.0,
     'q_nope_norm': 8.0,
     'q_rope_norm': 8.0}
    for name, (base, spread) in spreads.items():
        noise = np.random.default_rng([zlib.crc32(name.encode()), seed]).standard_normal(out[name].shape)
        drawn = base * np.exp(spread * noise) if base else spread * noise
        out[name] = __import__('jax').numpy.asarray(drawn.astype(out[name].dtype))
    for name, factor in factors.items():
        out[name] = (out[name] * factor).astype(out[name].dtype)
    return out
```

```python
import math
from contextlib import ExitStack, contextmanager

import numpy as np

import concourse.bass as bass
from concourse import mybir

F32, F32R, BF16, I32 = mybir.dt.float32, mybir.dt.float32r, mybir.dt.bfloat16, mybir.dt.int32
ALU, ACT, AX = mybir.AluOpType, mybir.ActivationFunctionType, mybir.AxisListType

P = 128
TOK, NT = 256, 2
D = 2048
KT = D // P
D_FF = 4 * D
PLE = 256
EPS = 1e-6
D_INNER, HEADS, HDIM, GROUPS, STATE, CONV_W = 2 * D, 64, 64, 8, 128, 4
GW = D_INNER // GROUPS
GH = HEADS // GROUPS
GN = GROUPS * STATE
CONV_TILES = (D_INNER + 2 * GN) // P
COL_Z, COL_X, COL_B = 0, D_INNER, 2 * D_INNER
COL_DT = 2 * D_INNER + 2 * GN
MH, NOPE, ROPE, VH, LORA = 16, 128, 64, 128, 512
QH = NOPE + ROPE
HALF = ROPE // 2
QUADS, QUAD = 4, 4
THETA = 10000.0
SCALE = float(QH) ** -0.5
NB = D // 512
RAW, SPL = 8, 4
MASKED = -1e30
TINY = 1e-30
CHUNK = 64
SCRATCH = 8960
STAT = 80
PI_IN = 3.1415925
HADDS = 2 * (4 * NB + NB) + (GROUPS + 1) * NB

V_MIX, V_MLP, V_PLE, V_KVIN, V_CKV, V_CQ, V_KN, V_QN = 0, 32, 64, 96, 112, 116, 120, 121
V_CONV = 128
V_SSM = 384
DT, DA, NCS, WGT, SKIP = 0, 2, 4, 6, 8


class Walk:

    def __init__(self, eng):
        self.eng, self.k, self.i, self.per = eng, {}, None, {}
        self.busy = {}

    def at(self, name, k, div=1):
        step = self.per.get(name.rstrip("'"), 0) // div
        return k // div if self.i is None or not step else self.i * step + k // div

    def tick(self, name):
        k = self.k.get(name, 0)
        self.k[name] = k + 1
        return k

    def now(self, name, less=0):
        return self.at(name, self.k.get(name, 0) - less)

    def skip(self, name, n=1):
        self.k[name] = self.k.get(name, 0) + n

    @contextmanager
    def rounds(self, count, per):
        start, held = dict(self.k), dict(self.busy)
        with self.eng.Fori(0, count) as i:
            self.i, self.per = i, per
            yield i
        for name in set(per) | set(self.k):
            met, one = self.k.get(name, 0) - start.get(name, 0), per.get(name.rstrip("'"), 0)
            assert met in (0, one), (name, met, one)
            self.k[name] = start.get(name, 0) + count * one
        for banks, (name, k) in self.busy.items():
            if held.get(banks) == (name, k):
                continue
            assert (name, k) == (held[banks][0], held[banks][1] + per[name]), (banks, name, k, held[banks])
            self.busy[banks] = name, k + (count - 1) * per[name]
        self.i, self.per = None, {}



MLP_ROUND = {"G": 64, "act": 4, "ahi": 4, "Tu": 4, "r": 4, "sq": 4, "hadd": 4, "dv": 0, "ac": 0}
SSD_ROUND = {"G": 24, "hadd": 4, "act": 1, "ahi": 1, "gp": 1, "gc": 1, "Tb": 1, "xd": 1, "seg": 2, "ex": 2,
             "Tcb": 1, "off": 1, "mm": 1, "Ty": 1, "yg": 1, "ys": 1, "yr": 1, "yn": 1, "Tyt": 1, "tm": 1,
             "xr": 1, "sz": 1, "Tc": 1, "c0": 1, "cv": 1, "si": 1, "dv": 5, "ac": 0}
QUAD_ROUND = {"G": 8, "ev": 4, "st": 1, "qrs": 2, "qn": 1, "Tq": 3, "qt": 3, "sc": 4, "mx": 4, "pe": 4,
              "pn": 4, "Tpt": 4, "ptc": 4, "To": 4, "ahi": 4, "act": 4, "dv": 18, "ac": 0}


def trunk_kernel(nc, x, p, positions, ln_mix, ln_mlp, mlp_w1, mlp_w2, ple_norm, ple_gate_w, ple_proj_w,
                 ssm_in_w, ssm_conv_w, ssm_conv_b, ssm_dt_bias, ssm_a_log, ssm_d, ssm_norm, ssm_out_w,
                 kv_in_norm, w_dkv, ckv_norm, w_kr, w_uk, w_uv, k_nope_norm, k_rope_norm,
                 w_dq, cq_norm, w_uq, q_nope_norm, q_rope_norm, mla_out_w, out):
    ctx = ExitStack()
    with ctx:
        def sb(name, shape, dt=F32):
            return ctx.enter_context(nc.sbuf_tensor(name, shape, dt))

        def sem(name):
            return ctx.enter_context(nc.semaphore(name))

        h = sb("h", [P, NT, D])
        xa = sb("xa_hi", [P, KT, TOK], F32R), sb("xa_lo", [P, KT, TOK], F32R)
        ya = sb("ya_hi", [P, KT, TOK], F32R), sb("ya_lo", [P, KT, TOK], F32R)
        raw = sb("raw", [P, RAW, 2, 512])
        w_hi, w_lo = sb("w_hi", [P, SPL, 2, 512], F32R), sb("w_lo", [P, SPL, 2, 512], F32R)
        pt = sb("pt_hi", [P, 2, TOK], F32R), sb("pt_lo", [P, 2, TOK], F32R)
        ident, upper = sb("ident", [P, P]), sb("upper", [P, P])
        identb, maskb = sb("identb", [P, P], BF16), sb("maskb", [P, P], BF16)
        amask = sb("amask", [P, 3 * P], BF16)
        vt = sb("vt", [P, 4 * P])
        bc = sb("bc", [P, 5, 64])
        hq = sb("hq", [P, 10, HEADS])
        cos, sin = sb("cos", [P, NT, HALF]), sb("sin", [P, NT, HALF])
        ssq, rstd = sb("ssq", [P, 6, NT, NB]), sb("rstd", [P, 6, NT])
        power = sb("power", [P, 6, 16])
        r_sb, sq_sb, tmp = sb("r_sb", [P, NT, 512]), sb("sq_sb", [P, NT, 512]), sb("tmp", [P, 4, TOK])
        junk = sb("junk", [P, NT, 512], BF16)
        small = sb("small", [P, 96])
        pos_i = sb("pos_i", [P, NT], I32)
        scratch = sb("scratch", [P, SCRATCH])

        at = [0]

        def part(*shape):
            n, a = math.prod(shape), at[0]
            at[0] += n
            assert at[0] <= SCRATCH, at
            v = scratch[:, a:a + n]
            if len(shape) == 2:
                return v.rearrange("p (a b) -> p a b", a=shape[0])
            if len(shape) == 3:
                return v.rearrange("p (a b c) -> p a b c", a=shape[0], b=shape[1])
            return v

        bct = part(2, GROUPS, TOK)
        late = at[0]
        dec = [part(GH, P), part(GH, P)]
        xdt = part(NT, GH, HDIM)
        sz = part(NT, 512)
        bg, cbo = part(2, TOK), part(P)
        hqg, gng, gcv, ysum, yroot = part(10, GH), part(4), part(5, 4), part(NT), part(NT)
        xs_t = r_sb[:, :, :].rearrange("p t n -> p (t n)").rearrange("p (a b) -> p a b", a=4)
        y4 = sq_sb[:, :, :].rearrange("p t (h d) -> p t h d", h=GH)
        xw = tmp[:, 0:2, :].rearrange("p a b -> p (a b)").rearrange("p (a b) -> p a b", a=GH)
        carried = tmp[:, 2:4, :].rearrange("p a b -> p (a b)").rearrange("p (a b) -> p a b", a=GH)
        at[0] = 0
        vrows, pos_f, freq = part(4, P), part(NT), part(HALF)
        ang, turns = part(NT, HALF), part(NT, HALF)
        at[0] = late
        pad = [part(NT, HEADS) for _ in range(4)]
        at[0] = 0
        prj, p_sb = part(NT, D), part(NT, PLE)
        at[0] = 0
        qf, sqf = part(NT, QUAD * QH), part(NT, QUAD * QH)
        q8, sq8 = (v.rearrange("p t n -> p (t n)").rearrange("p (n d) -> p n d", d=QH) for v in (qf, sqf))
        ktm, vtm = part(NT, 512), part(NT, 512)
        k_t, q_t = (v[:, :, :].rearrange("p t n -> p (t n)").rearrange("p (a b) -> p a b", a=QUAD)
                    for v in (r_sb, sq_sb))
        qr_t = tmp[:, :, :]
        qrp, kr_t = part(NT * QUAD, P), part(TOK)
        prob = [part(3 * P), part(3 * P)]
        prob_t = part(3 * P)
        kr_tm, krp = part(NT, ROPE), part(NT, P)

        bank = [ctx.enter_context(nc.psum_tensor(f"acc{n}", [P, 512], F32)) for n in range(4)]
        acc = {"A": bank[0:2], "B": bank[2:4]}
        tp = ctx.enter_context(nc.psum_tensor("tp", [P, 4, TOK], F32))
        mid = [ctx.enter_context(nc.psum_tensor(f"mid{n}", [P, 512], F32)) for n in range(2)]
        tflat = tp[:, :, :].rearrange("p a b -> p (a b)")
        ttok = tflat.rearrange("p (t n) -> p t n", t=NT)
        tbank = tflat[:, 0:512]

        s_raw = [sem(f"loaded{n}") for n in range(RAW)]
        S = {n: sem(n) for n in (
            "hi",
            "lo",
            "used",
            "ahi",
            "act",
            "tm",
            "Th",
            "Tu",
            "Tp",
            "r",
            "sq",
            "hadd",
            "sums",
            "rs",
            "dv", "ac", "po",
            "setup", "vec", "loads", "xin", "pin", "Tv", "vt", "rope_arg", "rope",
            "dt_x", "dt_e", "dt_u", "dt_ln", "dt_a", "Tcs", "dt_w", "dt_exp",
            "xr",
            "Tc",
            "gc",
            "c0",
            "cv",
            "si",
            "gp",
            "Tb",
            "xd",
            "seg",
            "ex",
            "Tcb",
            "off",
            "mm",
            "Ty",
            "sz",
            "yg",
            "ys",
            "yr",
            "yn",
            "Tyt",
            "pj",
            "gs",
            "outd",
            "ev",
            "csq",
            "crs",
            "cn",
            "Tkr",
            "krt",
            "st", "qrs",
            "qn",
            "Tq", "qt",
            "sc",
            "mx",
            "pe",
            "pn",
            "Tpt", "ptc",
            "To")}

        block = ctx.enter_context(nc.Block())
        taps_t = vt[:, V_CONV:V_CONV + 5 * CONV_TILES].rearrange("p (k c) -> p k c", k=CONV_W + 1)
        in_w, out_w = ssm_in_w[0], ssm_out_w[0]

        def c512(start):
            return slice(start, start + 512)

        def row_tiles(weight):
            return weight.rearrange("(r p) n -> p r n", p=P)

        def narrow(v):
            return v.rearrange("p k n -> p (k n)").rearrange("p (k n) -> p k n", n=64)

        @block.sync
        def _(sp):
            w = Walk(sp)

            def load(view, dst=lambda v: v):
                g = w.tick("G")
                if g >= RAW:
                    sp.wait_ge(S["lo"], w.at("G", g - RAW + 1))
                sp.dma_start(dst(raw[:, g % RAW]), view).then_inc(s_raw[g % RAW], 16)

            def unit(weight, cols, r0=0):
                v = row_tiles(weight)
                for k in range(KT // 2):
                    load(v[:, bass.ds(r0 + 2 * k, 2), cols])

            def rows4(weight, r0):
                v = row_tiles(weight)
                for n in range(NB):
                    for k in range(2):
                        load(v[:, bass.ds(r0 + 2 * k, 2), c512(512 * n)])

            load(row_tiles(in_w)[:, :, COL_DT:COL_DT + HEADS], narrow)
            for n in range(4):
                unit(in_w, c512(COL_B + 512 * n))
            for g in range(2):
                unit(in_w, c512(COL_X + GW * g))
                unit(in_w, c512(COL_Z + GW * g))
            with w.rounds(GROUPS - 2, SSD_ROUND) as i:
                rows4(out_w, i * 4)
                unit(in_w, bass.ds(i * GW + (COL_X + 2 * GW), 512))
                unit(in_w, bass.ds(i * GW + (COL_Z + 2 * GW), 512))
            for g in range(GROUPS - 2, GROUPS):
                rows4(out_w, 4 * g)

            def mlp(layer):
                up, down = mlp_w1[layer], mlp_w2[layer]
                unit(up, c512(0))
                with w.rounds(3, MLP_ROUND) as q:
                    for j in range(1, 4):
                        unit(up, bass.ds(q * D + 512 * j, 512))
                    for n in range(NB):
                        unit(down, c512(512 * n), q * KT)
                    unit(up, bass.ds(q * D + D, 512))
                for j in range(1, 4):
                    unit(up, c512(3 * D + 512 * j))
                for n in range(NB):
                    unit(down, c512(512 * n), 3 * KT)

            def gates(layer):
                v = row_tiles(ple_proj_w[layer])
                for n in range(NB):
                    load(v[:, :, c512(512 * n)])
                for n in range(NB):
                    unit(ple_gate_w[layer], c512(512 * n))

            mlp(0)
            gates(0)
            unit(w_dq[0], c512(0))
            unit(w_dkv, c512(0))
            load(row_tiles(w_kr), narrow)
            uq, uk, uv = row_tiles(w_uq[0]), row_tiles(w_uk), row_tiles(w_uv)
            with w.rounds(QUADS, QUAD_ROUND) as i:
                for pair in range(2):
                    for k in range(2):
                        load(uq[:, 2 * k:2 * k + 2, bass.ds(i * (QUAD * QH) + 2 * QH * pair, 2 * QH)],
                             lambda v: v[:, :, 0:2 * QH])
                for v in (uk, uv):
                    for k in range(2):
                        load(v[:, 2 * k:2 * k + 2, bass.ds(i * 512, 512)])
            for n in range(NB):
                unit(mla_out_w[0], c512(512 * n))
            mlp(1)
            gates(1)

        @block.gpsimd
        def _(pool):
            w = Walk(pool)

            def own(ins):
                ins.then_inc(S["po"], 1)
                w.tick("po")
                pool.wait_ge(S["po"], w.now("po"))

            values = (-0.5, EPS, 1.0 / D, 1.0 / LORA, 1.0 / NOPE, 1.0 / ROPE)
            for n, v in enumerate(values):
                pool.memset(power[:, n], v)
            pool.memset(upper[:, :], 1.0)
            pool.memset(ident[:, :], 0.0)
            pool.memset(identb[:, :], 0.0)
            pool.memset(maskb[:, :], 0.0)
            pool.memset(amask[:, :], 0.0)
            for n in range(HALF):
                pool.memset(freq[:, n:n + 1], float(np.float32(THETA) ** np.float32(-n / HALF)))
            own(pool.memset(vrows, 0.0))
            pool.affine_select(out=ident[:, :], in_=ident[:, :], compare_op=ALU.not_equal, fill=1.0,
                               base=0, pattern=[[-1, P]], channel_multiplier=1)
            pool.affine_select(out=identb[:, :], in_=identb[:, :], compare_op=ALU.not_equal, fill=1.0,
                               base=0, pattern=[[-1, P]], channel_multiplier=1)
            pool.affine_select(out=upper[:, :], in_=upper[:, :], compare_op=ALU.is_ge, fill=0.0,
                               base=0, pattern=[[1, P]], channel_multiplier=-1)
            pool.affine_select(out=maskb[:, :], in_=maskb[:, :], compare_op=ALU.is_ge, fill=MASKED,
                               base=0, pattern=[[1, P]], channel_multiplier=-1)
            pool.memset(amask[0:CHUNK, CHUNK:P], MASKED)
            pool.memset(amask[0:CHUNK, 3 * P - CHUNK:3 * P], MASKED).then_inc(S["setup"], 1)

            def rows(column, vec):
                pool.dma_start(vrows[column % P:column % P + vec.shape[0], column // P], vec)\
                    .then_inc(S["vec"], 16)

            def row128(v):
                return v.rearrange("(a b) -> a b", b=P)

            rows(V_MIX, ln_mix.rearrange("l (a b) -> (l a) b", b=P))
            rows(V_MLP, ln_mlp.rearrange("l (a b) -> (l a) b", b=P))
            rows(V_PLE, ple_norm.rearrange("l (a b) -> (l a) b", b=P))
            rows(V_KVIN, row128(kv_in_norm))
            rows(V_CKV, row128(ckv_norm))
            rows(V_CQ, row128(cq_norm[0]))
            rows(V_KN, row128(k_nope_norm))
            rows(V_QN, row128(q_nope_norm[0]))
            taps = ssm_conv_w[0].rearrange("k (a b) -> (k a) b", b=P)
            rows(V_CONV, taps[0:P])
            rows(V_CONV + P, taps[P:CONV_W * CONV_TILES])
            rows(V_CONV + CONV_W * CONV_TILES, row128(ssm_conv_b[0]))
            rows(V_SSM, row128(ssm_norm[0]))

            def root(src, n, dst):
                m = dst.shape[1]
                own(pool.tensor_tensor(dst, src, power[:, values.index(1.0 / n), 0:m], ALU.mult))
                own(pool.tensor_tensor(dst, dst, power[:, 1, 0:m], ALU.add))
                return pool.tensor_tensor(dst, dst, power[:, 0, 0:m], ALU.pow)

            def stream_root(n):
                pool.wait_ge(S["sums"], (n + 1) * NB)
                s = ssq[:, n]
                own(pool.tensor_tensor(s[:, :, 0:2], s[:, :, 0:2], s[:, :, 2:4], ALU.add))
                own(pool.tensor_tensor(rstd[:, n], s[:, :, 0], s[:, :, 1], ALU.add))
                root(rstd[:, n], D, rstd[:, n]).then_inc(S["rs"], 1)

            stream_root(0)
            pool.wait_ge(S["vt"], 1)
            pool.wait_ge(S["dt_exp"], 1)
            pool.wait_ge(S["si"], 4)
            with w.rounds(GROUPS, {"po": 2}) as i:
                pool.wait_ge(S["cv"], i + 4)
                pool.tensor_copy(gcv, taps_t[:, :, bass.ds(i * 4, 4)]).then_inc(S["gc"], 1)
                pool.wait_ge(S["tm"], i + NB)
                pool.tensor_copy(bg, bct[:, :, bass.ds(i, 1), :].rearrange("p a o t -> p (a o) t"))
                pool.tensor_copy(hqg, hq[:, :, bass.ds(i * GH, GH)])
                pool.tensor_copy(gng, vt[:, bass.ds(i * 4 + V_SSM, 4)]).then_inc(S["gp"], 1)
                pool.wait_ge(S["ys"], i + 1)
                root(ysum, GW, yroot).then_inc(S["yr"], 1)
            for n in (1, 2, 3):
                stream_root(n)
            pool.wait_ge(S["csq"], 1)
            root(small[:, 0:2], LORA, small[:, 6:8]).then_inc(S["crs"], 1)
            pool.wait_ge(S["csq"], 2)
            root(small[:, 2:4], LORA, small[:, 8:10]).then_inc(S["crs"], 1)
            pool.wait_ge(S["csq"], 3)
            root(small[:, 4:6], ROPE, small[:, 10:12]).then_inc(S["crs"], 1)
            with w.rounds(QUADS, {"po": 4}) as i:
                pool.wait_ge(S["st"], i + 1)
                root(small[:, 16:32], NOPE, small[:, 48:64]).then_inc(S["qrs"], 1)
                root(small[:, 32:40], ROPE, small[:, 64:72]).then_inc(S["qrs"], 1)
            for n in (4, 5):
                stream_root(n)
            o = out[0].rearrange("(t p) n -> p t n", p=P)
            for n in range(NB):
                pool.wait_ge(S["hadd"], HADDS - NB + 1 + n)
                pool.dma_start(o[:, :, c512(512 * n)], h[:, :, c512(512 * n)]).then_inc(S["outd"], 16)
            pool.wait_ge(S["outd"], 16 * NB)

        @block.scalar
        def _(act):
            w = Walk(act)

            def own(ins):
                ins.then_inc(S["ac"], 1)
                w.tick("ac")
                act.wait_ge(S["ac"], w.now("ac"))

            def split(cols=512):
                g = w.tick("G")
                act.wait_ge(s_raw[g % RAW], w.at("G", g, RAW) * 16 + 16)
                if g >= SPL:
                    act.wait_ge(S["used"], w.at("G", g - SPL + 1))
                act.activation(w_hi[:, g % SPL, :, 0:cols], raw[:, g % RAW, :, 0:cols], ACT.Copy)\
                    .then_inc(S["hi"], 1)

            def unit(jobs=None, halves=8, cols=512):
                before = w.k.get("G", 0)
                for n in range(halves):
                    split(cols)
                    for job in (jobs or {}).get(n, ()):
                        job(before)

            def take(dst, pair, signal, func=ACT.Copy, n=None, late=0, root=None):
                def job(before):
                    act.wait_ge(S["used"], w.at("G", before + late))
                    for t in range(NT):
                        scale = 1.0 if n is None else rstd[:, n, t:t + 1]
                        last = act.activation(dst(t), acc[pair][t][:, 0:dst(t).free_size()], func, scale=scale)
                    w.tick(signal)
                    last.then_inc(S[signal], 1)
                return job

            def act_hi(dst, src=None, event=None):
                def job(before=None):
                    name = event or "tm"
                    act.wait_ge(S[name], w.at(name, w.tick(name) + 1))
                    w.tick("ahi")
                    act.activation(dst, tmp[:, :, :] if src is None else src, ACT.Copy)\
                        .then_inc(S["ahi"], 1)
                return job

            def squares(src, dst, signal):
                if "junk" in w.busy:
                    name, k = w.busy["junk"]
                    act.wait_ge(S[name], w.at(name, k))
                w.busy["junk"] = signal, w.tick(signal) + 1
                for t in range(NT):
                    last = act.activation(junk[:, t, 0:src(t).free_size()], src(t), ACT.Square, accum_out=dst(t))
                last.then_inc(S[signal], 1)

            def sums(n, blk, event="hadd"):
                def job(before=None):
                    if event == "hadd":
                        act.wait_ge(S["hadd"], w.at("hadd", w.tick("hadd") + 1))
                    squares(lambda t: h[:, t, c512(512 * blk)], lambda t: ssq[:, n, t, blk:blk + 1], "sums")
                return job

            def tiles(dst, blk):
                return dst[0][:, 4 * blk:4 * blk + 4]

            for t in range(NT):
                act.dma_start(h[:, t], x[0, t * P:(t + 1) * P, :]).then_inc(S["xin"], 16)
            for n, v in enumerate((ssm_dt_bias[0], ssm_a_log[0], ssm_d[0], q_rope_norm[0], k_rope_norm)):
                act.dma_start(bc[:, n], v.partition_broadcast(P)).then_inc(S["loads"], 16)
            act.dma_start(pos_i[:, :], positions[0].rearrange("(t p) -> p t", p=P),
                          allow_slow_non_contiguous=True).then_inc(S["loads"], 16)
            act.wait_ge(S["xin"], 16 * NT)
            for blk in range(NB):
                sums(0, blk, None)()
            for blk in range(NB):
                act_hi(tiles(xa, blk))()
            act.wait_ge(S["rope_arg"], 1)
            act.activation(sin[:, :, :], ang, ACT.Sin)
            act.activation(cos[:, :, :], turns, ACT.Sin).then_inc(S["rope"], 1)
            act.wait_ge(S["rs"], 1)
            split()

            def softplus(before):
                act.wait_ge(S["dt_x"], 1)
                act.activation(pad[1], pad[1], ACT.Exp)
                act.activation(bc[:, 1], bc[:, 1], ACT.Exp).then_inc(S["dt_e"], 1)
                act.wait_ge(S["dt_u"], 1)
                act.activation(pad[3], pad[2], ACT.Ln).then_inc(S["dt_ln"], 1)

            def weights(before):
                act.wait_ge(S["dt_w"], 1)
                act.activation(hq[:, WGT:WGT + 2], pad[0], ACT.Exp).then_inc(S["dt_exp"], 1)

            def rows_out(pair, after_x=False):
                rows = take(lambda t: r_sb[:, t], pair, "xr", n=0)

                def job(before):
                    if after_x:
                        act.wait_ge(S["Tb"], w.at("Tb", w.tick("Tb") + 1))
                    rows(before)
                return job

            def conv_first(taps):
                def job(before=None):
                    act.wait_ge(S["Tc"], w.at("Tc", w.tick("Tc") + 1))
                    if taps is gcv:
                        act.wait_ge(S["gc"], w.at("gc", w.tick("gc") + 1))
                    for j in range(4):
                        last = act.activation(tmp[:, j], tp[:, j], ACT.Identity,
                                              scale=taps[:, CONV_W - 1, j:j + 1],
                                              bias=taps[:, CONV_W, j:j + 1])
                    w.tick("c0")
                    last.then_inc(S["c0"], 1)
                return job

            def conv_silu(dst):
                def job(before=None):
                    act.wait_ge(S["cv"], w.at("cv", w.tick("cv") + 1))
                    w.tick("si")
                    act.activation(dst, tmp[:, :, :], ACT.Silu).then_inc(S["si"], 1)
                return job

            def decays(b):
                def job(before=None):
                    act.wait_ge(S["seg"], w.at("seg", w.tick("seg") + 1))
                    if b == 0:
                        act.wait_ge(S["gp"], w.at("gp", w.tick("gp") + 1))
                    for n in range(GH):
                        last = act.activation(dec[b][:, n], mid[n // 4][:, P * (n % 4):P * (n % 4) + P],
                                              ACT.Exp, bias=hqg[:, NCS + b, n:n + 1])
                    w.tick("ex")
                    last.then_inc(S["ex"], 1)
                return job

            def cb_between(before=None):
                act.wait_ge(S["Tcb"], w.at("Tcb", w.tick("Tcb") + 1))
                w.tick("off")
                act.activation(cbo, tflat[:, P:2 * P], ACT.Copy).then_inc(S["off"], 1)

            def y_sums(before=None):
                act.wait_ge(S["yg"], w.at("yg", w.tick("yg") + 1))
                squares(lambda t: sq_sb[:, t], lambda t: ysum[:, t:t + 1], "ys")

            gate_z = take(lambda t: sz[:, t], "A", "sz", func=ACT.Silu, n=0)

            def conv_jobs(pair, taps, dst):
                return {3: [rows_out(pair)], 5: [conv_first(taps)], 7: [conv_silu(dst)]}

            static = taps_t[:, :, D_INNER // P:]
            unit({0: [softplus], 2: [weights]})
            for n in range(4):
                unit(conv_jobs("BA"[n % 2], static[:, :, 4 * n:4 * n + 4],
                               bct[:, n // 2, 4 * (n % 2):4 * (n % 2) + 4]))
            unit(conv_jobs("B", gcv, xs_t))
            unit({3: [gate_z], 5: [decays(0)], 7: [cb_between]})
            unit({0: [decays(1)], 4: [rows_out("B", True)],
                  7: [y_sums, act_hi(tiles(ya, 0)), conv_first(gcv), conv_silu(xs_t)]})
            with w.rounds(GROUPS - 2, SSD_ROUND):
                unit({3: [gate_z], 6: [decays(0)]})
                unit({0: [cb_between], 1: [decays(1)], 7: [y_sums]})
                unit({3: [act_hi(tiles(ya, 0))], 4: [rows_out("B", True)], 6: [conv_first(gcv)],
                      7: [conv_silu(xs_t)]})
            unit({3: [gate_z], 6: [decays(0)]})
            w.skip("hadd", 4)
            unit({0: [cb_between], 1: [decays(1)], 3: [y_sums, act_hi(tiles(ya, 0))],
                  7: [sums(1, 0), act_hi(tiles(xa, 0))]})

            def mlp(layer, pp, first):
                n = 1 + 3 * layer
                src = tp[:, :, :]

                def middle(pair, j):
                    return {3: [take(lambda t: r_sb[:, t], pair, "r", ACT.Relu, n)],
                            5: [act_hi(tiles(ya, j), src, "Tu")]}

                unit(first)
                act.wait_ge(S["rs"], n + 1)
                with w.rounds(3, MLP_ROUND):
                    for j in range(4):
                        unit(middle(pp[j % 2], j))
                    for j in range(4):
                        unit()
                for j in range(4):
                    unit(middle(pp[j % 2], j))
                act.dma_start(p_sb, p[layer, 0].rearrange("(t p) n -> p t n", p=P)).then_inc(S["pin"], 16)
                for j in range(3):
                    jobs = {5: [sums(n + 1, j), act_hi(tiles(xa, j))]}
                    if j == 2:
                        jobs[0] = [act_hi(pt[0][:, :, :], tp[:, 0:2, :], "Tp")]
                    unit(jobs)

            def gates(layer, pp):
                n = 2 + 3 * layer

                def product(j):
                    return take(lambda t: prj[:, t, c512(512 * j)], pp[j % 2], "pj", late=j + 1)

                def gate(j):
                    take_gate = take(lambda t: r_sb[:, t], pp[j % 2], "gs", ACT.Sigmoid, n)

                    def job(before):
                        if layer and j:
                            act.wait_ge(S["hadd"], w.at("hadd", w.tick("hadd") + 1))
                        take_gate(before)
                    return job

                def own_before(job, back):
                    return lambda before: job(before - back)

                unit({3: [product(0)]}, halves=4)
                jobs = {m: [own_before(product(m + 1), 4)] for m in range(3)}
                jobs[3] = [sums(n, 3), act_hi(tiles(xa, 3))]
                unit(jobs)
                act.wait_ge(S["rs"], n + 1)
                for j in range(3):
                    jobs = {3: [gate(j)]}
                    if layer == 0:
                        jobs[6] = [sums(n + 1, j), act_hi(tiles(ya, j))]
                    unit(jobs)
                if layer == 0:
                    unit({3: [gate(3)], 6: [sums(n + 1, 3), act_hi(tiles(ya, 3))]})
                else:
                    gate(3)(w.k["G"])

            mlp(0, "BA", {1: [sums(1, 1), act_hi(tiles(xa, 1))], 3: [sums(1, 2), act_hi(tiles(xa, 2))],
                          5: [sums(1, 3), act_hi(tiles(xa, 3))]})
            gates(0, "BA")

            def take_c(dst, pair, col, late=0):
                def job(before):
                    act.wait_ge(S["rs"], 4)
                    take(dst, pair, "ev", n=3, late=late)(before)
                    act.wait_ge(S["ev"], w.now("ev"))
                    squares(dst, lambda t: small[:, col + t:col + t + 1], "csq")
                return job

            unit({0: [act_hi(tiles(xa, 0))], 2: [act_hi(tiles(xa, 1))],
                  3: [take_c(lambda t: r_sb[:, t], "B", 0)],
                  4: [act_hi(tiles(xa, 2))], 6: [act_hi(tiles(xa, 3))]})
            unit({0: [take_c(lambda t: sq_sb[:, t], "A", 2),
                      take_c(lambda t: kr_tm[:, t], "B", 4, late=1),
                      act_hi(tiles(xa, 0)), act_hi(tiles(xa, 1))]}, halves=1)
            act.wait_ge(S["Tkr"], 1)
            act.activation(kr_t, tflat[:, 0:TOK], ACT.Copy).then_inc(S["krt"], 1)

            def copied(dst, gain):
                act.wait_ge(S["Tq"], w.at("Tq", w.tick("Tq") + 1))
                w.tick("qt")
                act.activation(dst, tp[:, :, :], ACT.Copy, scale=gain).then_inc(S["qt"], 1)

            def exps(j):
                act.wait_ge(S["mx"], w.at("mx", w.tick("mx") + 1))
                b = STAT + 8 * (j % 2)
                act.activation(prob[j % 2][:, 0:P], mid[j % 2][:, 0:P], ACT.Exp, scale=SCALE,
                               bias=small[:, b + 2:b + 3], accum_out=small[:, b + 4:b + 5])
                w.tick("pe")
                act.activation(prob[j % 2][:, P:3 * P], mid[j % 2][:, P:3 * P], ACT.Exp, scale=SCALE,
                               bias=small[:, b + 3:b + 4], accum_out=small[:, b + 5:b + 6])\
                    .then_inc(S["pe"], 1)

            def prob_copy():
                act.wait_ge(S["Tpt"], w.at("Tpt", w.tick("Tpt") + 1))
                w.tick("ptc")
                act.activation(prob_t, tflat[:, 0:3 * P], ACT.Copy).then_inc(S["ptc"], 1)

            with w.rounds(QUADS, QUAD_ROUND) as i:
                start = w.k["G"]
                q_of = lambda pair: lambda t: qf[:, t, 2 * QH * pair:2 * QH * (pair + 1)]
                unit(halves=4, cols=2 * QH)
                take(q_of(0), "A", "ev", late=2)(start)
                split()
                take(q_of(1), "B", "ev", late=4)(start)
                for n in range(3):
                    split()
                take(lambda t: ktm[:, t], "A", "ev", late=6)(start)
                take(lambda t: vtm[:, t], "B", "ev", late=8)(start)
                copied(k_t, vt[:, V_KN:V_KN + 1])
                copied(q_t, vt[:, V_QN:V_QN + 1])
                copied(qr_t, 1.0)

                def out_hi(j):
                    act_hi(ya[0][:, bass.ds(i * QUAD + j, 1)], tflat[:, 0:TOK], "To")()

                exps(0)
                exps(1)
                for j in range(QUAD):
                    prob_copy()
                    out_hi(j)
                    if j + 2 < QUAD:
                        exps(j + 2)
            unit()
            for j in range(3):
                unit({5: [sums(4, j), act_hi(tiles(xa, j))]})
            mlp(1, "AB", {5: [sums(4, 3), act_hi(tiles(xa, 3))]})
            gates(1, "AB")

        @block.vector
        def _(dve):
            w = Walk(dve)

            def own(ins):
                ins.then_inc(S["dv"], 1)
                w.tick("dv")
                dve.wait_ge(S["dv"], w.now("dv"))

            def on(event, n=None):
                dve.wait_ge(S[event], w.at(event, w.tick(event) + 1))

            def signal(ins, event):
                w.tick(event)
                ins.then_inc(S[event], 1)

            def rest(cols=512):
                g = w.tick("G")
                dve.wait_ge(S["hi"], w.at("G", g + 1))
                dve.tensor_tensor(w_lo[:, g % SPL, :, 0:cols], raw[:, g % RAW, :, 0:cols],
                                  w_hi[:, g % SPL, :, 0:cols].bitcast(F32), ALU.subtract).then_inc(S["lo"], 1)

            def unit(jobs=None, halves=8, cols=512):
                before = w.k.get("G", 0)
                for n in range(halves):
                    rest(cols)
                    for job in (jobs or {}).get(n, ()):
                        job(before)

            def tiles(dst, blk):
                return dst[0][:, 4 * blk:4 * blk + 4], dst[1][:, 4 * blk:4 * blk + 4]

            def lo(dst, src=None):
                def job(before=None):
                    on("ahi")
                    signal(dve.tensor_tensor(dst[1], tmp[:, :, :] if src is None else src,
                                             dst[0].bitcast(F32), ALU.subtract), "act")
                return job

            def gain(col, event="Th"):
                def job(before=None):
                    on(event)
                    g = gng if col is None else vt[:, col:col + 4]
                    signal(dve.tensor_tensor(tmp[:, :, :], tp[:, :, :],
                                             g.unsqueeze(2).to_broadcast([P, 4, TOK]), ALU.mult), "tm")
                return job

            def add(pair, blk, late=0):
                def job(before):
                    dve.wait_ge(S["used"], w.at("G", before + late))
                    for t in range(NT):
                        v = h[:, t, c512(512 * blk)]
                        last = dve.tensor_tensor(v, acc[pair][t][:, :], v, ALU.add)
                    signal(last, "hadd")
                return job

            on("Tv")
            dve.tensor_copy(vt[:, :], tbank).then_inc(S["vt"], 1)
            for blk in range(NB):
                gain(V_MIX + 4 * blk)()
                lo(tiles(xa, blk))()
            dve.wait_ge(S["loads"], 16 * 6)
            own(dve.tensor_copy(pos_f, pos_i[:, :]))
            for t in range(NT):
                last = dve.tensor_scalar(ang[:, t], freq, pos_f[:, t:t + 1], None, ALU.mult)
            own(last)
            magic = 1.5 * 2.0 ** 23
            own(dve.tensor_scalar(turns, ang, 1.0 / (2 * math.pi), magic, ALU.mult, ALU.add))
            own(dve.tensor_scalar(turns, turns, magic, None, ALU.subtract))
            rest_of = 2 * math.pi
            for bits in (5, 14, 23, 34):
                c = round(rest_of * 2 ** bits) / 2 ** bits
                rest_of -= c
                own(dve.scalar_tensor_tensor(ang, turns, -c, ang, ALU.mult, ALU.add))
            own(dve.tensor_scalar(ang, ang, PI_IN, -PI_IN, ALU.min, ALU.max))
            own(dve.scalar_tensor_tensor(turns, ang, -1.0, ang, ALU.mult, ALU.max))
            dve.tensor_scalar(turns, turns, -1.0, math.pi / 2, ALU.mult, ALU.add).then_inc(S["rope_arg"], 1)
            dve.wait_ge(S["rs"], 1)
            rest()
            dve.wait_ge(S["used"], 1)
            for t in range(NT):
                last = dve.scalar_tensor_tensor(pad[0][:, t], acc["A"][t][:, 0:HEADS], rstd[:, 0, t:t + 1],
                                                bc[:, 0], ALU.mult, ALU.add)
            own(last)
            dve.scalar_tensor_tensor(pad[1], pad[0], -1.0, pad[0], ALU.mult, ALU.min).then_inc(S["dt_x"], 1)

            def dt_log(before):
                dve.wait_ge(S["dt_e"], 1)
                own(dve.tensor_scalar(pad[2], pad[1], 1.0, None, ALU.add))
                dve.tensor_scalar(hq[:, WGT:WGT + 2], pad[2], -1.0, TINY, ALU.add, ALU.add).then_inc(S["dt_u"], 1)
                dve.wait_ge(S["dt_u"], 1)
                own(dve.reciprocal(hq[:, WGT:WGT + 2], hq[:, WGT:WGT + 2]))
                own(dve.tensor_tensor(pad[1], pad[1], hq[:, WGT:WGT + 2], ALU.mult))
                dve.wait_ge(S["dt_ln"], 1)
                own(dve.scalar_tensor_tensor(pad[1], pad[3], TINY, pad[1], ALU.add, ALU.mult))
                own(dve.scalar_tensor_tensor(hq[:, DT:DT + 2], pad[0], 0.0, pad[1], ALU.max, ALU.add))
                dve.scalar_tensor_tensor(hq[:, DA:DA + 2], hq[:, DT:DT + 2], -1.0,
                                         bc[:, 1].unsqueeze(1).to_broadcast([P, NT, HEADS]),
                                         ALU.mult, ALU.mult).then_inc(S["dt_a"], 1)

            def dt_sums(before):
                dve.wait_ge(S["Tcs"], 1)
                cs = tbank[:, 0:NT * HEADS].rearrange("p (t n) -> p t n", t=NT)
                for t in range(NT):
                    dve.tensor_copy(hq[:, SKIP + t], bc[:, 2])
                own(dve.tensor_scalar(hq[:, NCS:NCS + 2], cs, -1.0, None, ALU.mult))
                dve.tensor_tensor(pad[0][:, 0], tbank[:, 2 * HEADS:3 * HEADS], hq[:, NCS], ALU.add)
                dve.tensor_copy(pad[0][:, 1], cs[:, 1]).then_inc(S["dt_w"], 1)

            def conv_taps(taps, lags):
                def job(before=None):
                    if lags[0] == 1:
                        on("c0")
                    for d in lags:
                        for j in range(4):
                            v = tmp[:, j, d:TOK]
                            last = dve.scalar_tensor_tensor(v, tp[:, j, 0:TOK - d],
                                                            taps[:, CONV_W - 1 - d, j:j + 1], v,
                                                            ALU.mult, ALU.add)
                        if d < lags[-1]:
                            own(last)
                    if lags[-1] == CONV_W - 1:
                        signal(last, "cv")
                    else:
                        own(last)
                return job

            def heads(v, kind):
                return hqg[:, kind].unsqueeze(2).to_broadcast([P, GH, HDIM])

            def x_dt(before=None):
                on("gp")
                on("Tb")
                for t in range(NT):
                    v = ttok[:, t].rearrange("p (h d) -> p h d", h=GH)
                    last = dve.tensor_tensor(xdt[:, t], v, heads(v, DT + t), ALU.mult)
                    dve.tensor_tensor(y4[:, t], v, heads(v, SKIP + t), ALU.mult)
                own(last)
                signal(dve.tensor_tensor(xw, xdt[:, 0], heads(xw, WGT), ALU.mult), "xd")

            def decay_cb(b):
                def job(before=None):
                    on("ex")
                    if b == 0:
                        on("off")
                    v = tflat[:, 2 * P * b:2 * P * b + P].unsqueeze(1).to_broadcast([P, GH, P])
                    last = dve.tensor_tensor(dec[b], v, dec[b], ALU.mult)
                    if b == 1:
                        signal(last, "mm")
                return job

            def y_gate(before=None):
                on("Ty")
                dve.tensor_tensor(carried, tbank.rearrange("p (h d) -> p h d", h=GH),
                                  heads(carried, WGT + 1), ALU.mult)
                for t in range(NT):
                    last = dve.tensor_tensor(sq_sb[:, t], mid[t][:, :], sq_sb[:, t], ALU.add)
                own(last)
                own(dve.tensor_tensor(y4[:, 1], y4[:, 1], carried, ALU.add))
                on("sz")
                signal(dve.tensor_tensor(sq_sb[:, :, :], sq_sb[:, :, :], sz, ALU.mult), "yg")

            def y_norm(before=None):
                on("yr")
                for t in range(NT):
                    last = dve.tensor_scalar(sq_sb[:, t], sq_sb[:, t], yroot[:, t:t + 1], None, ALU.mult)
                signal(last, "yn")

            def y_gain(before=None):
                gain(None, "Tyt")()

            def y_lo(before=None):
                lo(tiles(ya, 0))()
                
            static = taps_t[:, :, D_INNER // P:]
            unit({0: [dt_log], 2: [dt_sums]})
            for n in range(4):
                unit({6: [conv_taps(static[:, :, 4 * n:4 * n + 4], (1, 2, 3))]})
            unit({6: [conv_taps(gcv, (1, 2, 3))]})
            unit({4: [x_dt]})
            unit({0: [decay_cb(0)], 2: [decay_cb(1)], 4: [y_gate],
                  7: [y_norm, y_gain, y_lo, conv_taps(gcv, (1, 2, 3))]})
            def before_out(job):
                return lambda before: job(before - 8)

            with w.rounds(GROUPS - 2, SSD_ROUND):
                unit({5: [add("B", 0, 2)], 6: [x_dt], 7: [add("A", 1, 4)]})
                unit({0: [decay_cb(0)], 1: [before_out(add("B", 2, 6))], 2: [decay_cb(1)],
                      3: [before_out(add("A", 3, 8))], 5: [y_gate]})
                unit({0: [y_norm], 2: [y_gain], 3: [y_lo], 7: [conv_taps(gcv, (1, 2, 3))]})
            unit({5: [add("B", 0, 2)], 6: [x_dt], 7: [add("A", 1, 4)]})
            unit({0: [decay_cb(0)], 1: [before_out(add("B", 2, 6))], 2: [decay_cb(1)],
                  3: [before_out(add("A", 3, 8)), y_gate, y_norm, y_gain, y_lo],
                  5: [add("B", 0, 2)], 7: [gain(V_MLP), add("A", 1, 4)]})

            def mlp(layer, pp, first):
                def middle(pair, j):
                    def square(before):
                        on("r")
                        signal(dve.tensor_tensor(sq_sb[:, :, :], r_sb[:, :, :], r_sb[:, :, :], ALU.mult), "sq")
                    return {3: [square], 5: [lo(tiles(ya, j), tp[:, :, :])]}

                unit(first)
                with w.rounds(3, MLP_ROUND):
                    for j in range(4):
                        unit(middle(pp[j % 2], j))
                    for j in range(4):
                        unit({3: [add(pp[j % 2], j)]})
                for j in range(4):
                    unit(middle(pp[j % 2], j))
                for j in range(3):
                    jobs = {3: [add(pp[j % 2], j)], 5: [gain(V_PLE + 16 * layer + 4 * j)], 6: [lo(tiles(xa, j))]}
                    if j == 2:
                        jobs[0] = [lo((pt[0][:, :, :], pt[1][:, :, :]), tp[:, 0:2, :])]
                    unit(jobs)

            def gates(layer, pp):
                def gated(j):
                    def job(before):
                        on("gs")
                        if j == 0:
                            dve.wait_ge(S["pj"], 4 * layer + 4)
                        own(dve.tensor_tensor(r_sb[:, :, :], r_sb[:, :, :], prj[:, :, c512(512 * j)], ALU.mult))
                        v = h[:, :, c512(512 * j)]
                        signal(dve.tensor_tensor(v, v, r_sb[:, :, :], ALU.add), "hadd")
                    return job

                unit({3: [add(pp[1], 3)]}, halves=4)
                unit({1: [gain(V_PLE + 16 * layer + 12)], 4: [lo(tiles(xa, 3))]})
                for j in range(3):
                    jobs = {3: [gated(j)]}
                    if layer == 0:
                        jobs[6] = [gain(V_MIX + 16 + 4 * j)]
                        jobs[7] = [lo(tiles(ya, j))]
                    unit(jobs)
                if layer == 0:
                    unit({3: [gated(3)], 6: [gain(V_MIX + 16 + 12)], 7: [lo(tiles(ya, 3))]})
                else:
                    gated(3)(None)

            add_out = lambda n: before_out(add("BA"[n % 2], n, 2 * n + 2))
            mlp(0, "BA", {0: [lo(tiles(xa, 0))], 1: [gain(V_MLP + 4), add_out(2)], 2: [lo(tiles(xa, 1))],
                          3: [gain(V_MLP + 8), add_out(3)], 4: [lo(tiles(xa, 2))],
                          5: [gain(V_MLP + 12)], 6: [lo(tiles(xa, 3))]})
            gates(0, "BA")
            kv = lambda j: gain(V_KVIN + 4 * j)
            unit({n: [kv(n // 2) if n % 2 == 0 else lo(tiles(xa, n // 2))] for n in range(8)})
            rest()
            dve.memset(krp, 0.0)
            own(dve.memset(qrp, 0.0))

            def normalised(v, col, n):
                dve.wait_ge(S["crs"], n)
                for t in range(NT):
                    last = dve.tensor_scalar(v[:, t], v[:, t], small[:, col + t:col + t + 1], None, ALU.mult)
                return last

            normalised(r_sb, 6, 1).then_inc(S["cn"], 1)
            normalised(sq_sb, 8, 2).then_inc(S["cn"], 1)
            gain(V_CQ)()
            lo(tiles(xa, 0))()
            dve.wait_ge(S["rope"], 1)

            def rotate(dst, v, cs, sn, a, b):
                own(dve.tensor_tensor(a, v[0], cs, ALU.mult))
                own(dve.tensor_tensor(b, v[1], sn, ALU.mult))
                own(dve.tensor_tensor(dst[0], a, b, ALU.subtract))
                own(dve.tensor_tensor(a, v[1], cs, ALU.mult))
                own(dve.tensor_tensor(b, v[0], sn, ALU.mult))
                return dve.tensor_tensor(dst[1], a, b, ALU.add)

            own(normalised(kr_tm, 10, 3))
            own(dve.tensor_tensor(kr_tm, kr_tm, bc[:, 4].unsqueeze(1).to_broadcast([P, NT, ROPE]), ALU.mult))
            two = lambda v: (v[:, :, 0:HALF], v[:, :, HALF:ROPE])
            pad_a, pad_b = sqf[:, 0, 0:NT * HALF], sqf[:, 1, 0:NT * HALF]
            pad_a, pad_b = (v.rearrange("p (a b) -> p a b", a=NT) for v in (pad_a, pad_b))
            rotate(two(krp), two(kr_tm), cos[:, :, :], sin[:, :, :], pad_a, pad_b).then_inc(S["cn"], 1)
            gain(V_CKV)()
            lo(tiles(xa, 1))()

            NH = NT * QUAD
            w.skip("ev", 3)
            with w.rounds(QUADS, QUAD_ROUND) as i:
                unit(halves=4, cols=2 * QH)
                unit(halves=4)
                on("ev")
                on("ev")
                own(dve.tensor_tensor(sqf, qf, qf, ALU.mult))
                dve.tensor_reduce(small[:, 16:24], sq8[:, :, 0:NOPE], AX.X, ALU.add)
                own(dve.tensor_reduce(small[:, 32:40], sq8[:, :, NOPE:QH], AX.X, ALU.add))
                on("ev")
                sk = sqf[:, :, 0:512]
                own(dve.tensor_tensor(sk, ktm, ktm, ALU.mult))
                on("ev")
                signal(dve.tensor_reduce(small[:, 24:32].rearrange("p (t n) -> p t n", t=NT),
                                         sk.rearrange("p t (n d) -> p t n d", d=NOPE), AX.X, ALU.add), "st")
                on("qrs")
                on("qrs")
                k8 = ktm.rearrange("p t n -> p (t n)").rearrange("p (n d) -> p n d", d=NOPE)
                dve.tensor_tensor(k8, k8, small[:, 56:64].unsqueeze(2).to_broadcast([P, NH, NOPE]), ALU.mult)
                qn = q8[:, :, 0:NOPE]
                dve.tensor_tensor(qn, qn, small[:, 48:56].unsqueeze(2).to_broadcast([P, NH, NOPE]), ALU.mult)
                qr = q8[:, :, NOPE:QH]
                own(dve.tensor_tensor(qr, qr, small[:, 64:72].unsqueeze(2).to_broadcast([P, NH, ROPE]), ALU.mult))
                own(dve.tensor_tensor(qr, qr, bc[:, 3].unsqueeze(1).to_broadcast([P, NH, ROPE]), ALU.mult))
                q4 = qf.rearrange("p t (n d) -> p t n d", d=QH)
                qrp4 = qrp.rearrange("p (t n) d -> p t n d", t=NT)
                half_a = [v[:, :, :, 0:HALF] for v in (q4[:, :, :, NOPE:QH], qrp4)]
                half_b = [v[:, :, :, HALF:ROPE] for v in (q4[:, :, :, NOPE:QH], qrp4)]
                spread = lambda v: v[:, :, :].unsqueeze(2).to_broadcast([P, NT, QUAD, HALF])
                pads = [sqf[:, n].rearrange("p (t n d) -> p t n d", t=NT, d=QH // 2)[:, :, :, 0:HALF] for n in range(2)]
                signal(rotate((half_a[1], half_b[1]), (half_a[0], half_b[0]), spread(cos), spread(sin),
                              pads[0], pads[1]), "qn")

                def maxima(j):
                    on("sc")
                    b = STAT + 8 * (j % 2)
                    dve.tensor_reduce(small[:, b:b + 1], mid[j % 2][:, 0:P], AX.X, ALU.max)
                    own(dve.tensor_reduce(small[:, b + 1:b + 2], mid[j % 2][:, P:3 * P], AX.X, ALU.max))
                    signal(dve.tensor_scalar(small[:, b + 2:b + 4], small[:, b:b + 2], -SCALE, None, ALU.mult), "mx")

                def probabilities(j):
                    on("pe")
                    b = STAT + 8 * (j % 2)
                    own(dve.reciprocal(small[:, b + 6:b + 8], small[:, b + 4:b + 6]))
                    v = prob[j % 2]
                    dve.tensor_scalar(v[:, 0:P], v[:, 0:P], small[:, b + 6:b + 7], None, ALU.mult)
                    signal(dve.tensor_scalar(v[:, P:3 * P], v[:, P:3 * P], small[:, b + 7:b + 8], None, ALU.mult), "pn")

                def out_lo(j):
                    at_ = bass.ds(i * QUAD + j, 1)
                    lo((ya[0][:, at_], ya[1][:, at_]), tflat[:, 0:TOK].unsqueeze(1))()

                maxima(0)
                maxima(1)
                probabilities(0)
                probabilities(1)
                out_lo(0)
                maxima(2)
                out_lo(1)
                maxima(3)
                probabilities(2)
                out_lo(2)
                probabilities(3)
                out_lo(3)
            unit()
            for j in range(3):
                unit({3: [add("AB"[j % 2], j)], 5: [gain(V_MLP + 16 + 4 * j)], 6: [lo(tiles(xa, j))]})
            mlp(1, "AB", {3: [add("B", 3)], 5: [gain(V_MLP + 28)], 6: [lo(tiles(xa, 3))]})
            gates(1, "AB")

        @block.tensor
        def _(pe):
            w = Walk(pe)

            def hold(banks, event):
                for b in banks:
                    if b in w.busy:
                        name, k = w.busy[b]
                        pe.wait_ge(S[name], w.at(name, k))
                k = w.tick(event) + 1
                for b in banks:
                    w.busy[b] = event, k

            def on(event):
                pe.wait_ge(S[event], w.at(event + "'", w.tick(event + "'") + 1))

            def chunk(x, tile, pair, first, last, cols=512, view=None, k_n=2, signal=True):
                g = w.tick("G")
                pe.wait_ge(S["lo"], w.at("G", g + 1))
                hi, lo_ = w_hi[:, g % SPL], w_lo[:, g % SPL]
                if view:
                    hi, lo_ = view(hi), view(lo_)
                for k in range(k_n):
                    for t in range(NT):
                        rows = slice(t * P, t * P + P)
                        dst = acc[pair][t][:, 0:cols]
                        xh, xl = x[0][:, tile + k, rows], x[1][:, tile + k, rows]
                        wh, wl = hi[:, k, 0:cols], lo_[:, k, 0:cols]
                        pe.matmul(dst, xh, wh, start=first and k == 0, stop=False)
                        pe.matmul(dst, xh, wl, start=False, stop=False)
                        mm = pe.matmul(dst, xl, wh, start=False, stop=last and k == k_n - 1)
                mm.then_inc(S["used"], 1)

            def unit(x, pair, event, jobs=None, need=None):
                hold(pair, event)
                for n in range(8):
                    if need and n % 2 == 0:
                        pe.wait_ge(S["act"], w.at("act", need[n // 2]))
                    chunk(x, 2 * n, pair, n == 0, n == 7)
                    for job in (jobs or {}).get(n, ()):
                        job()

            def flip(src, per, n, m):
                for j in range(n):
                    for t in range(m):
                        last = pe.transpose(per(j, t), src(j, t), ident[:, :])
                return last

            def feature(j, t):
                return tp[:, j, t * P:t * P + P]

            def turn_h(blk, updates):
                def job():
                    if updates:
                        pe.wait_ge(S["hadd"], updates)
                    hold("T", "act")
                    flip(lambda j, t: h[:, t, 512 * blk + P * j:512 * blk + P * j + P], feature, 4, NT)\
                        .then_inc(S["Th"], 1)
                return job

            pe.wait_ge(S["setup"], 1)
            pe.wait_ge(S["vec"], 16 * 12)
            hold("T", "vt")
            for n in range(4):
                last = pe.transpose(tbank[:, n * P:(n + 1) * P], vrows[:, n], ident[:, :])
            last.then_inc(S["Tv"], 1)
            pe.wait_ge(S["xin"], 16 * NT)
            for blk in range(NB):
                turn_h(blk, 0)()
            pe.wait_ge(S["act"], NB)
            hold("A", "dt_x")
            chunk(xa, 0, "A", True, True, HEADS, narrow, KT)

            def cumulative():
                pe.wait_ge(S["dt_a"], 1)
                hold("T", "dt_w")
                for t in range(NT):
                    pe.matmul(tbank[:, t * HEADS:(t + 1) * HEADS], upper[:, :], hq[:, DA + t], start=True, stop=True)
                pe.matmul(tbank[:, NT * HEADS:(NT + 1) * HEADS], upper[:, P - 1:P].to_broadcast([P, P]),
                          hq[:, DA], start=True, stop=True).then_inc(S["Tcs"], 1)

            def turn_rows():
                on("xr")
                hold("T", "cv")
                flip(lambda j, t: r_sb[:, t, P * j:P * j + P], feature, 4, NT).then_inc(S["Tc"], 1)

            def turn_back():
                on("si")
                hold("T", "xd")
                flip(lambda j, t: xs_t[:, j, t * P:t * P + P], lambda j, t: ttok[:, t, P * j:P * j + P], 4, NT)\
                    .then_inc(S["Tb"], 1)

            def exponents(b):
                def job():
                    if b == 0:
                        on("gp")
                    hold("M", "ex")
                    for m in range(2):
                        pe.matmul(mid[m][:, :], identb[:, :], maskb[:, :].unsqueeze(1).to_broadcast([P, 4, P]),
                                  start=True, stop=False)
                        for n in range(4):
                            a = hqg[:, DA + b, 4 * m + n:4 * m + n + 1].to_broadcast([P, P])
                            last = pe.matmul(mid[m][:, n * P:n * P + P], a, upper[:, :], start=False, stop=n == 3)
                    last.then_inc(S["seg"], 1)
                return job

            def c_b():
                hold("T", "mm")
                pe.matmul(tflat[:, 0:TOK], bg[:, 0, 0:P], bg[:, 1, :], start=True, stop=True)
                pe.matmul(tflat[:, TOK:TOK + P], bg[:, 0, P:TOK], bg[:, 1, P:TOK], start=True, stop=True)\
                    .then_inc(S["Tcb"], 1)

            def y_products():
                hold(("T", "M"), "yg")
                for b in range(NT):
                    for n in range(GH):
                        pe.matmul(mid[b][:, HDIM * n:HDIM * n + HDIM], dec[b][:, n], xdt[:, b, n],
                                  start=True, stop=True)
                pe.matmul(tbank, cbo, xw.rearrange("p h d -> p (h d)"), start=True, stop=True)\
                    .then_inc(S["Ty"], 1)

            def turn_y():
                on("yn")
                hold("T", "act")
                flip(lambda j, t: sq_sb[:, t, P * j:P * j + P], feature, 4, NT).then_inc(S["Tyt"], 1)

            def out_piece(jobs, pairs):
                pe.wait_ge(S["act"], w.now("act"))
                for n in range(NB):
                    hold(pairs[n % 2], "hadd")
                    for k in range(2):
                        chunk(ya, 2 * k, pairs[n % 2], k == 0, k == 1)
                        for job in jobs.get(2 * n + k, ()):
                            job()

            unit(xa, "B", "xr", {1: [cumulative]})
            for n in range(3):
                unit(xa, "AB"[n % 2], "xr", {1: [turn_rows]})
            unit(xa, "B", "xr", {1: [turn_rows]})
            w.skip("si'", 4)
            unit(xa, "A", "sz", {1: [turn_rows]})
            unit(xa, "B", "xr", {0: [turn_back], 1: [exponents(0)], 3: [c_b], 4: [exponents(1)], 7: [y_products]})
            unit(xa, "A", "sz", {4: [turn_y], 6: [turn_rows]})
            with w.rounds(GROUPS - 2, SSD_ROUND):
                out_piece({1: [turn_back], 2: [exponents(0)], 4: [c_b], 5: [exponents(1)]}, "BA")
                unit(xa, "B", "xr", {0: [y_products], 6: [turn_y]})
                unit(xa, "A", "sz", {2: [turn_rows]})
            out_piece({1: [turn_back], 2: [exponents(0)], 4: [c_b], 5: [exponents(1)],
                       7: [y_products, turn_y]}, "BA")
            out_piece({3: [turn_h(0, 29)], 5: [turn_h(1, 30)], 7: [turn_h(2, 31)]}, "BA")

            def needs(posted):
                return [w.k["act"] - posted + 1 + n for n in range(4)]

            def mlp(layer, pp, last_turn):
                def turn_middle():
                    on("sq")
                    hold("T", "act")
                    flip(lambda j, t: sq_sb[:, t, P * j:P * j + P], feature, 4, NT).then_inc(S["Tu"], 1)

                def turn_p():
                    pe.wait_ge(S["pin"], 16 * (layer + 1))
                    hold("T", "act")
                    flip(lambda j, t: p_sb[:, t, P * j:P * j + P], feature, 2, NT).then_inc(S["Tp"], 1)

                base = 32 + 24 * layer + 12
                unit(xa, pp[0], "r", {1: [last_turn]}, needs(3))
                with w.rounds(3, MLP_ROUND):
                    for j in range(1, 4):
                        unit(xa, pp[j % 2], "r", {1: [turn_middle]})
                    unit(ya, pp[0], "hadd", {1: [turn_middle]}, needs(3))
                    for j in range(1, 4):
                        unit(ya, pp[j % 2], "hadd")
                    unit(xa, pp[0], "r")
                for j in range(1, 4):
                    unit(xa, pp[j % 2], "r", {1: [turn_middle]})
                unit(ya, pp[0], "hadd", {1: [turn_middle]}, needs(3))
                unit(ya, pp[1], "hadd", {1: [turn_h(0, base + 1)]})
                unit(ya, pp[0], "hadd", {1: [turn_h(1, base + 2)], 4: [turn_p]})
                unit(ya, pp[1], "hadd", {1: [turn_h(2, base + 3)]})
                c = w.k["act"]
                pe.wait_ge(S["act"], c - 1)
                for n in range(NB):
                    hold(pp[n % 2], "pj")
                    chunk(pt, 0, pp[n % 2], True, True)
                    if n == 1:
                        turn_h(3, base + 4)()
                jobs = lambda n, slot: {slot: [turn_h(n, base + 5 + n)]} if layer == 0 else {}
                unit(xa, pp[0], "gs", None, [c - 3, c - 2, c, c + 1])
                for n in range(3):
                    unit(xa, pp[(n + 1) % 2], "gs", jobs(n, 2))
                w.skip("hadd", NB)
                return base

            base = mlp(0, "BA", turn_h(3, 32))
            unit(ya, "B", "ev", {2: [turn_h(3, base + 8)], 4: [turn_h(0, 0)], 6: [turn_h(1, 0)]}, needs(3))
            unit(xa, "A", "ev", {0: [turn_h(2, 0)], 2: [turn_h(3, 0)]}, needs(2))
            hold("B", "ev")
            chunk(xa, 0, "B", True, True, ROPE, narrow, KT)
            for n, src in enumerate((r_sb, sq_sb)):
                pe.wait_ge(S["cn"], n + 1)
                hold("T", "act")
                flip(lambda j, t: src[:, t, P * j:P * j + P], feature, 4, NT).then_inc(S["Th"], 1)
            pe.wait_ge(S["cn"], 3)
            hold("T", "krt")
            flip(lambda j, t: krp[:, t], lambda j, t: tflat[:, t * P:t * P + P], 1, NT).then_inc(S["Tkr"], 1)
            pe.wait_ge(S["act"], w.k["act"])
            pe.wait_ge(S["krt"], 1)
            w.busy = {"T": ("act", w.k["act"])}
            with w.rounds(QUADS, QUAD_ROUND):
                pe.wait_ge(S["ev"], w.now("ev"))
                for n, (pair, tile, cols) in enumerate((("A", 0, 384), ("B", 0, 384), ("A", 4, 512), ("B", 4, 512))):
                    if n >= 2:
                        pe.wait_ge(S["ev"], w.at("ev", w.k["ev"] + n - 1))
                    for k in range(2):
                        chunk(xa, tile + 2 * k, pair, k == 0, k == 1, cols)
                w.skip("ev", 4)
                on("qn")
                k4 = ktm.rearrange("p t (n d) -> p t n d", d=NOPE)
                q4 = qf.rearrange("p t (n d) -> p t n d", d=QH)
                r4 = qrp.rearrange("p (t n) d -> p t n d", t=NT)
                for src in (k4, q4[:, :, :, 0:NOPE], r4):
                    hold("T", "qt")
                    flip(lambda j, t: src[:, t, j], feature, QUAD, NT).then_inc(S["Tq"], 1)

                def scores(j):
                    pe.wait_ge(S["pe"], w.now("pe", 0 if j < 2 else 1 - j))
                    if j == 0:
                        pe.wait_ge(S["qt"], w.now("qt"))
                    m = mid[j % 2]
                    pe.matmul(m[:, 0:3 * P], identb[:, :], amask[:, :], start=True, stop=False)
                    for t, (a, b) in enumerate(((0, P), (P, 3 * P))):
                        rows = slice(t * P, t * P + P)
                        pe.matmul(m[:, a:b], q_t[:, j, rows], k_t[:, j, 0:b - a], start=False, stop=False)
                        last = pe.matmul(m[:, a:b], qr_t[:, j, rows], kr_t[:, 0:b - a], start=False, stop=t == 1)
                    last.then_inc(S["sc"], 1)

                def weigh(j):
                    on("pn")
                    hold("T", "ptc")
                    for n in range(3):
                        last = pe.transpose(tflat[:, n * P:n * P + P], prob[j % 2][:, n * P:n * P + P], ident[:, :])
                    last.then_inc(S["Tpt"], 1)
                    hold("T", "act")
                    v = [vtm[:, t, j * VH:(j + 1) * VH] for t in range(NT)]
                    pe.matmul(tflat[:, 0:TOK], v[0], prob_t[:, 0:TOK], start=True, stop=False)
                    pe.matmul(tflat[:, P:TOK], v[1], prob_t[:, TOK:3 * P], start=False, stop=True)\
                        .then_inc(S["To"], 1)

                scores(0)
                scores(1)
                for j in range(QUAD):
                    weigh(j)
                    if j + 2 < QUAD:
                        scores(j + 2)
                w.skip("pe", 4)
            w.busy.update(A=("ev", w.k["ev"]), B=("ev", w.k["ev"]))
            pe.wait_ge(S["act"], w.k["act"])
            unit(ya, "A", "hadd")
            for j in range(3):
                unit(ya, "BA"[j % 2], "hadd", {1: [turn_h(j, 53 + j)]})
            mlp(1, "AB", turn_h(3, 56))
            

_INS = ["x", "p", "positions", "ln_mix", "ln_mlp", "mlp_w1", "mlp_w2", "ple_norm", "ple_gate_w", "ple_proj_w",
        "ssm_in_w", "ssm_conv_w", "ssm_conv_b", "ssm_dt_bias", "ssm_a_log", "ssm_d", "ssm_norm", "ssm_out_w",
        "kv_in_norm", "w_dkv", "ckv_norm", "w_kr", "w_uk", "w_uv", "k_nope_norm", "k_rope_norm",
        "w_dq", "cq_norm", "w_uq", "q_nope_norm", "q_rope_norm", "mla_out_w"]


def kernel(**inputs):
    import concourse.bacc as _bacc
    from concourse.bass_utils import run_bass_kernel_spmd as _run

    nc = _bacc.Bacc("TRN2", target_bir_lowering=False, num_devices=1)
    arrays, args = {}, []
    for name in _INS:
        a = np.ascontiguousarray(inputs[name])
        arrays[f"in_{name}"] = a
        args.append(nc.dram_tensor(f"in_{name}", a.shape, mybir.dt.from_np(a.dtype), kind="ExternalInput").ap())
    out = nc.dram_tensor("out_0", (1, TOK, D), F32, kind="ExternalOutput").ap()
    trunk_kernel(nc, *args, out)
    r = _run(nc, [arrays], core_ids=[0])
    return r.results[0]["out_0"]
```

```python
import math
from contextlib import ExitStack, contextmanager

import numpy as np

import concourse.bass as bass
from concourse import mybir

F32, F32R, BF16, I32 = mybir.dt.float32, mybir.dt.float32r, mybir.dt.bfloat16, mybir.dt.int32
ALU, ACT, AX = mybir.AluOpType, mybir.ActivationFunctionType, mybir.AxisListType

P = 128
TOK, NT = 256, 2
D = 2048
KT = D // P
D_FF = 4 * D
PLE = 256
EPS = 1e-6
D_INNER, HEADS, HDIM, GROUPS, STATE, CONV_W = 2 * D, 64, 64, 8, 128, 4
GW = D_INNER // GROUPS
GH = HEADS // GROUPS
GN = GROUPS * STATE
CONV_TILES = (D_INNER + 2 * GN) // P
COL_Z, COL_X, COL_B = 0, D_INNER, 2 * D_INNER
COL_DT = 2 * D_INNER + 2 * GN
MH, NOPE, ROPE, VH, LORA = 16, 128, 64, 128, 512
QH = NOPE + ROPE
HALF = ROPE // 2
QUADS, QUAD = 4, 4
THETA = 10000.0
SCALE = float(QH) ** -0.5
NB = D // 512
RAW, SPL = 8, 4
MASKED = -1e30
TINY = 1e-30
CHUNK = 64
SCRATCH = 9200
Q2 = QUAD * QH - 512
STAT = 80
PI_IN = 3.1415925
HADDS = 2 * (4 * NB + NB) + (GROUPS + 1) * NB

V_MIX, V_MLP, V_PLE, V_KVIN, V_CKV, V_CQ, V_KN, V_QN = 0, 32, 64, 96, 112, 116, 120, 121
V_CONV = 128
V_SSM = 384
V_ROWS = (V_QN + 1, P, (CONV_W + 1) * CONV_TILES - P, D_INNER // P)
DT, DA, NCS, WGT, SKIP = 0, 2, 4, 6, 8


class Walk:

    def __init__(self, eng):
        self.eng, self.k, self.i, self.per = eng, {}, None, {}
        self.busy = {}

    def at(self, name, k, div=1):
        step = self.per.get(name.rstrip("'"), 0) // div
        return k // div if self.i is None or not step else self.i * step + k // div

    def tick(self, name):
        k = self.k.get(name, 0)
        self.k[name] = k + 1
        return k

    def now(self, name, less=0):
        return self.at(name, self.k.get(name, 0) - less)

    def skip(self, name, n=1):
        self.k[name] = self.k.get(name, 0) + n

    @contextmanager
    def rounds(self, count, per):
        start, held = dict(self.k), dict(self.busy)
        with self.eng.Fori(0, count) as i:
            self.i, self.per = i, per
            yield i
        for name in set(per) | set(self.k):
            met, one = self.k.get(name, 0) - start.get(name, 0), per.get(name.rstrip("'"), 0)
            assert met in (0, one), (name, met, one)
            self.k[name] = start.get(name, 0) + count * one
        for banks, (name, k) in self.busy.items():
            if held.get(banks) == (name, k):
                continue
            assert (name, k) == (held[banks][0], held[banks][1] + per[name]), (banks, name, k, held[banks])
            self.busy[banks] = name, k + (count - 1) * per[name]
        self.i, self.per = None, {}


MLP_ROUND = {"G": 64, "act": 4, "ahi": 4, "Tu": 4, "r": 4, "sq": 4, "hadd": 4}
SSD_ROUND = {"G": 24, "hadd": 4, "act": 1, "ahi": 1, "gp": 1, "gc": 1, "Tb": 1, "xd": 1, "sg": 1, "ex": 1, "csb": 1,
             "Tcb": 1, "off": 1, "mm": 1, "Ty": 1, "yg": 1, "ys": 1, "yr": 1, "yn": 1, "Tyt": 1, "tm": 1,
             "xr": 1, "sz": 1, "Tc": 1, "c0": 1, "cv": 1, "si": 1, "dv": 6}
QUAD_ROUND = {"G": 8, "ev": 4, "st": 2, "qrs": 2, "qn": 1, "kn": 1, "qrot": 1, "hs": 2,
              "Tq": 3, "qt": 3, "sc": 4, "mx": 4, "pe": 4, "pn": 4, "Tpt": 4, "ptc": 4, "To": 4,
              "ahi": 4, "act": 4, "dv": 8}


def trunk_kernel(nc, x, p, positions, ln_mix, ln_mlp, mlp_w1, mlp_w2, ple_norm, ple_gate_w, ple_proj_w,
                 ssm_in_w, ssm_conv_w, ssm_conv_b, ssm_dt_bias, ssm_a_log, ssm_d, ssm_norm, ssm_out_w,
                 kv_in_norm, w_dkv, ckv_norm, w_kr, w_uk, w_uv, k_nope_norm, k_rope_norm,
                 w_dq, cq_norm, w_uq, q_nope_norm, q_rope_norm, mla_out_w, out):
    ctx = ExitStack()
    with ctx:
        def sb(name, shape, dt=F32):
            return ctx.enter_context(nc.sbuf_tensor(name, shape, dt))

        def sem(name):
            return ctx.enter_context(nc.semaphore(name))

        NH = NT * QUAD
        h = sb("h", [P, NT, D])
        xa = sb("xa_hi", [P, KT, TOK], F32R), sb("xa_lo", [P, KT, TOK], F32R)
        ya = sb("ya_hi", [P, KT, TOK], F32R), sb("ya_lo", [P, KT, TOK], F32R)
        raw = sb("raw", [P, RAW, 2, 512])
        w_hi, w_lo = sb("w_hi", [P, SPL, 2, 512], F32R), sb("w_lo", [P, SPL, 2, 512], F32R)
        pt = sb("pt_hi", [P, 2, TOK], F32R), sb("pt_lo", [P, 2, TOK], F32R)
        ident, upper = sb("ident", [P, P]), sb("upper", [P, P])
        identb = sb("identb", [P, P], BF16)
        amask = sb("amask", [P, 3 * P], BF16)
        vt = sb("vt", [P, 4 * P])
        bc = sb("bc", [P, 5, 64])
        hq = sb("hq", [P, 10, HEADS])
        cos, sin = sb("cos", [P, NT, HALF]), sb("sin", [P, NT, HALF])
        ssq, rstd = sb("ssq", [P, 6, NT, NB]), sb("rstd", [P, 6, NT])
        power = sb("power", [P, 6, 16])
        r_sb, sq_sb, tmp = sb("r_sb", [P, NT, 512]), sb("sq_sb", [P, NT, 512]), sb("tmp", [P, 4, TOK])
        junk = sb("junk", [P, NT, 512], BF16)
        small = sb("small", [P, 96])
        pos_i = sb("pos_i", [P, NT], I32)
        scratch = sb("scratch", [P, SCRATCH])

        at = [0]

        def part(*shape):
            n, a = math.prod(shape), at[0]
            at[0] += n
            assert at[0] <= SCRATCH, at
            v = scratch[:, a:a + n]
            if len(shape) == 2:
                return v.rearrange("p (a b) -> p a b", a=shape[0])
            if len(shape) == 3:
                return v.rearrange("p (a b c) -> p a b c", a=shape[0], b=shape[1])
            return v

        bct = part(2, GROUPS, TOK)
        late = at[0]
        dec_all = part(NT * GH * P)
        dec = [dec_all[:, b * GH * P:(b + 1) * GH * P].rearrange("p (h l) -> p h l", h=GH) for b in range(NT)]
        xdt = part(NT, GH, HDIM)
        sz = part(NT, 512)
        bg, cbo, cbd = part(2, TOK), part(P), part(NT, P)
        hqg, gng, gcv, ysum, yroot = part(10, GH), part(4), part(5, 4), part(NT), part(NT)
        xs_t = r_sb[:, :, :].rearrange("p t n -> p (t n)").rearrange("p (a b) -> p a b", a=4)
        y4 = sq_sb[:, :, :].rearrange("p t (h d) -> p t h d", h=GH)
        xw = tmp[:, 0:2, :].rearrange("p a b -> p (a b)").rearrange("p (a b) -> p a b", a=GH)
        carried = tmp[:, 2:4, :].rearrange("p a b -> p (a b)").rearrange("p (a b) -> p a b", a=GH)
        at[0] = 0
        vrows, pos_f, freq = part(4, P), part(NT), part(HALF)
        ang, turns = part(NT, HALF), part(NT, HALF)
        at[0] = late
        pad = [part(NT, HEADS) for _ in range(4)]
        at[0] = 0
        prj, p_sb = part(NT, D), part(NT, PLE)
        at[0] = 0
        qf, sqf = part(NT, QUAD * QH), part(NT, QUAD * QH)
        q8, sq8 = (v.rearrange("p t n -> p (t n)").rearrange("p (n d) -> p n d", d=QH) for v in (qf, sqf))
        ktm, vtm = part(NT, 512), part(NT, 512)
        k_t, q_t = (v[:, :, :].rearrange("p t n -> p (t n)").rearrange("p (a b) -> p a b", a=QUAD)
                    for v in (r_sb, sq_sb))
        qr_t = tmp[:, :, :]
        qrp, kr_t = part(NT * QUAD, P), part(TOK)
        prob = [part(3 * P), part(3 * P)]
        prob_t = part(3 * P)
        kr_tm, krp = part(NT, ROPE), part(NT, P)
        krow_t = sqf[0:ROPE, 0, 0:TOK]
        ksq = part(NT, 512)

        bank = [ctx.enter_context(nc.psum_tensor(f"acc{n}", [P, 512], F32)) for n in range(4)]
        acc = {"A": bank[0:2], "B": bank[2:4]}
        tp = ctx.enter_context(nc.psum_tensor("tp", [P, 4, TOK], F32))
        mid = [ctx.enter_context(nc.psum_tensor(f"mid{n}", [P, 512], F32)) for n in range(2)]
        tflat = tp[:, :, :].rearrange("p a b -> p (a b)")
        ttok = tflat.rearrange("p (t n) -> p t n", t=NT)
        tbank = tflat[:, 0:512]

        cs_t = sq_sb[0:HEADS, :, 0:P]
        cs_dram = nc.dram_tensor("cumulative", (NT, HEADS * P), F32, kind="Internal").ap()
        dt_t = r_sb[0:HEADS, 0, 0:TOK]
        pairs = lambda v: v[:, :].rearrange("p (a b) -> p a b", a=2)
        first_psum = ((tp[:, 0:2], tp[:, 2:4]), (pairs(mid[0]), pairs(mid[1])),
                      (pairs(bank[2]), pairs(bank[3])), (pairs(bank[0]), pairs(bank[1])))
        first_tmp = (tmp[:, :, :], k_t, q_t, tmp[:, :, :])

        s_raw = [sem(f"loaded{n}") for n in range(RAW)]
        S = {n: sem(n) for n in (
            "hi",
            "lo",
            "used",
            "ahi",
            "act",
            "tm",
            "Th",
            "Tu",
            "Tp",
            "r",
            "sq",
            "hadd",
            "sums",
            "rs",
            "dv", "po",
            "setup",
            "vec",
            "loads",
            "xin", "pin",
            "Tv", "vt",
            "rope_arg", "rope",
            "nt",
            "Tn",
            "dt_x", "dt_e",
            "dt_u", "dt_ln",
            "dt_a", "Tcs",
            "dt_w", "dt_exp",
            "xr",
            "Tc",
            "gc",
            "c0",
            "cv",
            "si",
            "gp",
            "Tb",
            "xd",
            "cst",
            "Tcst",
            "cs_out",
            "csb",
            "sg",
            "ex",
            "Tcb",
            "off",
            "mm",
            "Ty",
            "sz",
            "yg",
            "ys",
            "yr",
            "yn",
            "Tyt",
            "outd",
            "pj",
            "gs",
            "ev",
            "kt",
            "csq",
            "crs",
            "cn",
            "Tkr",
            "krt",
            "hs",
            "st", "qrs",
            "qn", "kn",
            "qrot",
            "Tq", "qt",
            "sc",
            "mx",
            "pe",
            "pn",
            "Tpt", "ptc",
            "To")}

        block = ctx.enter_context(nc.Block())
        taps_t = vt[:, V_CONV:V_CONV + 5 * CONV_TILES].rearrange("p (k c) -> p k c", k=CONV_W + 1)
        in_w, out_w = ssm_in_w[0], ssm_out_w[0]

        def c512(start):
            return slice(start, start + 512)

        def row_tiles(weight):
            return weight.rearrange("(r p) n -> p r n", p=P)

        def narrow(v):
            return v.rearrange("p k n -> p (k n)").rearrange("p (k n) -> p k n", n=64)

        @block.sync
        def _(sp):
            w = Walk(sp)

            def load(view, dst=lambda v: v):
                g = w.tick("G")
                if g >= RAW:
                    sp.wait_ge(S["lo"], w.at("G", g - RAW + 1))
                sp.dma_start(dst(raw[:, g % RAW]), view).then_inc(s_raw[g % RAW], 16)

            def unit(weight, cols, r0=0):
                v = row_tiles(weight)
                for k in range(KT // 2):
                    load(v[:, bass.ds(r0 + 2 * k, 2), cols])

            def rows4(weight, r0):
                v = row_tiles(weight)
                for n in range(NB):
                    for k in range(2):
                        load(v[:, bass.ds(r0 + 2 * k, 2), c512(512 * n)])

            def rows(column, vec):
                sp.dma_start(vrows[column % P:column % P + vec.shape[0], column // P], vec)\
                    .then_inc(S["vec"], 16)

            def row128(v):
                return v.rearrange("(a b) -> a b", b=P)

            rows(V_MIX, ln_mix.rearrange("l (a b) -> (l a) b", b=P))
            rows(V_MLP, ln_mlp.rearrange("l (a b) -> (l a) b", b=P))
            rows(V_PLE, ple_norm.rearrange("l (a b) -> (l a) b", b=P))
            rows(V_KVIN, row128(kv_in_norm))
            rows(V_CKV, row128(ckv_norm))
            rows(V_CQ, row128(cq_norm[0]))
            rows(V_KN, row128(k_nope_norm))
            rows(V_QN, row128(q_nope_norm[0]))
            taps = ssm_conv_w[0].rearrange("k (a b) -> (k a) b", b=P)
            rows(V_CONV, taps[0:P])
            rows(V_CONV + P, taps[P:CONV_W * CONV_TILES])
            rows(V_CONV + CONV_W * CONV_TILES, row128(ssm_conv_b[0]))
            rows(V_SSM, row128(ssm_norm[0]))
            load(row_tiles(in_w)[:, :, COL_DT:COL_DT + HEADS], narrow)
            for n in range(4):
                unit(in_w, c512(COL_B + 512 * n))
            for g in range(2):
                unit(in_w, c512(COL_X + GW * g))
                unit(in_w, c512(COL_Z + GW * g))
            with w.rounds(GROUPS - 2, SSD_ROUND) as i:
                rows4(out_w, i * 4)
                unit(in_w, bass.ds(i * GW + (COL_X + 2 * GW), 512))
                unit(in_w, bass.ds(i * GW + (COL_Z + 2 * GW), 512))
            for g in range(GROUPS - 2, GROUPS):
                rows4(out_w, 4 * g)

            def mlp(layer):
                up, down = mlp_w1[layer], mlp_w2[layer]
                unit(up, c512(0))
                with w.rounds(3, MLP_ROUND) as q:
                    for j in range(1, 4):
                        unit(up, bass.ds(q * D + 512 * j, 512))
                    for n in range(NB):
                        unit(down, c512(512 * n), q * KT)
                    unit(up, bass.ds(q * D + D, 512))
                for j in range(1, 4):
                    unit(up, c512(3 * D + 512 * j))
                for n in range(NB):
                    unit(down, c512(512 * n), 3 * KT)

            def gates(layer):
                v = row_tiles(ple_proj_w[layer])
                for n in range(NB):
                    load(v[:, :, c512(512 * n)])
                for n in range(NB):
                    unit(ple_gate_w[layer], c512(512 * n))

            mlp(0)
            gates(0)
            unit(w_dq[0], c512(0))
            unit(w_dkv, c512(0))
            load(row_tiles(w_kr), narrow)
            uq, uk, uv = row_tiles(w_uq[0]), row_tiles(w_uk), row_tiles(w_uv)

            def heads(i):
                for col, cols in ((0, 512), (512, Q2)):
                    for k in range(2):
                        load(uq[:, 2 * k:2 * k + 2, bass.ds(i * (QUAD * QH) + col, cols)],
                             lambda v, cols=cols: v[:, :, 0:cols])
                for v in (uk, uv):
                    for k in range(2):
                        load(v[:, 2 * k:2 * k + 2, bass.ds(i * 512, 512)])

            heads(0)
            with w.rounds(QUADS - 1, QUAD_ROUND) as i:
                heads(i + 1)
            v = row_tiles(mla_out_w[0])
            for tiles in (range(0, KT - QUAD, 2), range(KT - QUAD, KT, 2)):
                for n in range(2):
                    for k in tiles:
                        load(v[:, k:k + 2, c512(512 * n)])
            for n in range(2, NB):
                unit(mla_out_w[0], c512(512 * n))
            mlp(1)
            gates(1)

        @block.gpsimd
        def _(pool):
            w = Walk(pool)

            def own(ins):
                ins.then_inc(S["po"], 1)
                w.tick("po")
                pool.wait_ge(S["po"], w.now("po"))

            values = (-0.5, EPS, 1.0 / D, 1.0 / LORA, 1.0 / NOPE, 1.0 / ROPE)
            for n, v in enumerate(values):
                pool.memset(power[:, n], v)
            pool.memset(ident[:, :], 0.0)
            pool.memset(upper[:, :], 1.0)
            pool.memset(identb[:, :], 0.0)
            own(pool.memset(amask[:, :], 0.0))
            pool.affine_select(out=ident[:, :], in_=ident[:, :], compare_op=ALU.not_equal, fill=1.0,
                               base=0, pattern=[[-1, P]], channel_multiplier=1).then_inc(S["setup"], 1)
            pool.affine_select(out=identb[:, :], in_=identb[:, :], compare_op=ALU.not_equal, fill=1.0,
                               base=0, pattern=[[-1, P]], channel_multiplier=1)
            pool.affine_select(out=upper[:, :], in_=upper[:, :], compare_op=ALU.is_ge, fill=0.0,
                               base=0, pattern=[[1, P]], channel_multiplier=-1)
            pool.memset(amask[0:CHUNK, CHUNK:P], MASKED)
            pool.memset(amask[0:CHUNK, 3 * P - CHUNK:3 * P], MASKED)
            for n in range(HALF):
                last = pool.memset(freq[:, n:n + 1], float(np.float32(THETA) ** np.float32(-n / HALF)))
            last.then_inc(S["setup"], 1)

            def root(src, n, dst):
                m = dst.shape[1]
                own(pool.tensor_tensor(dst, src, power[:, values.index(1.0 / n), 0:m], ALU.mult))
                own(pool.tensor_tensor(dst, dst, power[:, 1, 0:m], ALU.add))
                return pool.tensor_tensor(dst, dst, power[:, 0, 0:m], ALU.pow)

            def stream_root(n):
                pool.wait_ge(S["sums"], (n + 1) * NB)
                s = ssq[:, n]
                own(pool.tensor_tensor(s[:, :, 0:2], s[:, :, 0:2], s[:, :, 2:4], ALU.add))
                own(pool.tensor_tensor(rstd[:, n], s[:, :, 0], s[:, :, 1], ALU.add))
                root(rstd[:, n], D, rstd[:, n]).then_inc(S["rs"], 1)

            stream_root(0)
            pool.wait_ge(S["vt"], 1)
            pool.wait_ge(S["dt_exp"], 1)
            pool.wait_ge(S["si"], 4)
            pool.wait_ge(S["cs_out"], 16 * NT)
            with w.rounds(GROUPS, {"po": 2}) as i:
                for b in range(NT):
                    pool.dma_start(dec_all[:, b * GH * P:(b + 1) * GH * P],
                                   cs_dram[b, bass.ds(i * (GH * P), GH * P)].partition_broadcast(P))\
                        .then_inc(S["csb"], 16)
                pool.wait_ge(S["cv"], i + 4)
                pool.tensor_copy(gcv, taps_t[:, :, bass.ds(i * 4, 4)]).then_inc(S["gc"], 1)
                pool.wait_ge(S["tm"], i + NB)
                pool.tensor_copy(bg, bct[:, :, bass.ds(i, 1), :].rearrange("p a o t -> p (a o) t"))
                pool.tensor_copy(hqg, hq[:, :, bass.ds(i * GH, GH)])
                pool.tensor_copy(gng, vt[:, bass.ds(i * 4 + V_SSM, 4)]).then_inc(S["gp"], 1)
                pool.wait_ge(S["ys"], i + 1)
                root(ysum, GW, yroot).then_inc(S["yr"], 1)
            for n in (1, 2, 3):
                stream_root(n)
            pool.wait_ge(S["csq"], 1)
            root(small[:, 0:2], LORA, small[:, 6:8]).then_inc(S["crs"], 1)
            pool.wait_ge(S["csq"], 2)
            root(small[:, 2:4], LORA, small[:, 8:10]).then_inc(S["crs"], 1)
            pool.wait_ge(S["csq"], 3)
            root(small[:, 4:6], ROPE, small[:, 10:12]).then_inc(S["crs"], 1)
            q4 = qf.rearrange("p t (n d) -> p t n d", d=QH)
            qrp4 = qrp.rearrange("p (t n) d -> p t n d", t=NT)
            spread = lambda v: v[:, :, :].unsqueeze(2).to_broadcast([P, NT, QUAD, HALF])
            with w.rounds(QUADS, {"po": 10}) as i:
                pool.wait_ge(S["st"], 2 * i + 1)
                root(small[:, 16:24], NOPE, small[:, 48:56]).then_inc(S["qrs"], 1)
                own(root(small[:, 32:40], ROPE, small[:, 64:72]))
                pool.wait_ge(S["st"], 2 * i + 2)
                root(small[:, 24:32], NOPE, small[:, 56:64]).then_inc(S["qrs"], 1)
                qr = q8[:, :, NOPE:QH]
                own(pool.tensor_tensor(qr, qr, small[:, 64:72].unsqueeze(2).to_broadcast([P, NH, ROPE]), ALU.mult))
                own(pool.tensor_tensor(qr, qr, bc[:, 3].unsqueeze(1).to_broadcast([P, NH, ROPE]), ALU.mult))
                a, b = q4[:, :, :, NOPE:NOPE + HALF], q4[:, :, :, NOPE + HALF:QH]
                pool.tensor_tensor(qrp4[:, :, :, 0:HALF], a, spread(cos), ALU.mult)
                pool.tensor_tensor(qrp4[:, :, :, HALF:ROPE], b, spread(cos), ALU.mult)
                pool.tensor_tensor(b, b, spread(sin), ALU.mult)
                own(pool.tensor_tensor(a, a, spread(sin), ALU.mult))
                pool.tensor_tensor(qrp4[:, :, :, 0:HALF], qrp4[:, :, :, 0:HALF], b, ALU.subtract)
                pool.tensor_tensor(qrp4[:, :, :, HALF:ROPE], qrp4[:, :, :, HALF:ROPE], a, ALU.add)\
                    .then_inc(S["qrot"], 1)
            for n in (4, 5):
                stream_root(n)
            o = out[0].rearrange("(t p) n -> p t n", p=P)
            for n in range(NB):
                pool.wait_ge(S["hadd"], HADDS - NB + 1 + n)
                pool.dma_start(o[:, :, c512(512 * n)], h[:, :, c512(512 * n)]).then_inc(S["outd"], 16)
            pool.wait_ge(S["outd"], 16 * NB)

        @block.scalar
        def _(act):
            w = Walk(act)

            def split(cols=512):
                g = w.tick("G")
                act.wait_ge(s_raw[g % RAW], w.at("G", g, RAW) * 16 + 16)
                if g >= SPL:
                    act.wait_ge(S["used"], w.at("G", g - SPL + 1))
                act.activation(w_hi[:, g % SPL, :, 0:cols], raw[:, g % RAW, :, 0:cols], ACT.Copy)\
                    .then_inc(S["hi"], 1)

            def unit(jobs=None, halves=8, cols=512):
                before = w.k.get("G", 0)
                for n in range(halves):
                    split(cols)
                    for job in (jobs or {}).get(n, ()):
                        job(before)

            def take(dst, pair, signal, func=ACT.Copy, n=None, late=0, root=None):
                def job(before):
                    act.wait_ge(S["used"], w.at("G", before + late))
                    for t in range(NT):
                        scale = 1.0 if n is None else rstd[:, n, t:t + 1]
                        last = act.activation(dst(t), acc[pair][t][:, 0:dst(t).free_size()], func, scale=scale)
                    w.tick(signal)
                    last.then_inc(S[signal], 1)
                return job

            def act_hi(dst, src=None, event=None):
                def job(before=None):
                    name = event or "tm"
                    act.wait_ge(S[name], w.at(name, w.tick(name) + 1))
                    w.tick("ahi")
                    act.activation(dst, tmp[:, :, :] if src is None else src, ACT.Copy)\
                        .then_inc(S["ahi"], 1)
                return job

            def squares(src, dst, signal):
                if "junk" in w.busy:
                    name, k = w.busy["junk"]
                    act.wait_ge(S[name], w.at(name, k))
                w.busy["junk"] = signal, w.tick(signal) + 1
                for t in range(NT):
                    last = act.activation(junk[:, t, 0:src(t).free_size()], src(t), ACT.Square, accum_out=dst(t))
                last.then_inc(S[signal], 1)

            def sums(n, blk, event="hadd"):
                def job(before=None):
                    if event == "hadd":
                        act.wait_ge(S["hadd"], w.at("hadd", w.tick("hadd") + 1))
                    squares(lambda t: h[:, t, c512(512 * blk)], lambda t: ssq[:, n, t, blk:blk + 1], "sums")
                return job

            def tiles(dst, blk):
                return dst[0][:, 4 * blk:4 * blk + 4]

            for t in range(NT):
                act.dma_start(h[:, t], x[0, t * P:(t + 1) * P, :]).then_inc(S["xin"], 16)
            for n, v in enumerate((ssm_dt_bias[0], ssm_a_log[0], ssm_d[0], q_rope_norm[0], k_rope_norm)):
                act.dma_start(bc[:, n], v.partition_broadcast(P)).then_inc(S["loads"], 16)
            act.dma_start(pos_i[:, :], positions[0].rearrange("(t p) -> p t", p=P),
                          allow_slow_non_contiguous=True).then_inc(S["loads"], 16)
            act.wait_ge(S["xin"], 16 * NT)
            for blk in range(NB):
                act_hi(tiles(xa, blk), first_tmp[blk])()
            split()
            for blk in range(NB):
                sums(0, blk, None)()

            def take_narrow(dst, pair, late=1):
                def job(before):
                    act.wait_ge(S["used"], before + late)
                    act.activation(dst, acc[pair][0][0:HEADS, 0:TOK], ACT.Copy).then_inc(S["nt"], 1)
                return job

            def rope_sines(before):
                act.wait_ge(S["rope_arg"], 1)
                act.activation(sin[:, :, :], ang, ACT.Sin)
                act.activation(cos[:, :, :], turns, ACT.Sin).then_inc(S["rope"], 1)
                act.wait_ge(S["rs"], 1)

            def softplus(before):
                act.wait_ge(S["dt_x"], 1)
                act.activation(pad[1], pad[1], ACT.Exp)
                act.activation(bc[:, 1], bc[:, 1], ACT.Exp).then_inc(S["dt_e"], 1)
                act.wait_ge(S["dt_u"], 1)
                act.activation(pad[3], pad[2], ACT.Ln).then_inc(S["dt_ln"], 1)

            def weights(before):
                act.wait_ge(S["dt_w"], 1)
                act.activation(hq[:, WGT:WGT + 2], pad[0], ACT.Exp).then_inc(S["dt_exp"], 1)

            def rows_out(pair, after_x=False):
                rows = take(lambda t: r_sb[:, t], pair, "xr", n=0)

                def job(before):
                    if after_x:
                        act.wait_ge(S["Tb"], w.at("Tb", w.tick("Tb") + 1))
                    rows(before)
                return job

            def conv_first(taps):
                def job(before=None):
                    act.wait_ge(S["Tc"], w.at("Tc", w.tick("Tc") + 1))
                    if taps is gcv:
                        act.wait_ge(S["gc"], w.at("gc", w.tick("gc") + 1))
                    for j in range(4):
                        last = act.activation(tmp[:, j], tp[:, j], ACT.Identity,
                                              scale=taps[:, CONV_W - 1, j:j + 1],
                                              bias=taps[:, CONV_W, j:j + 1])
                    w.tick("c0")
                    last.then_inc(S["c0"], 1)
                return job

            def conv_silu(dst):
                def job(before=None):
                    act.wait_ge(S["cv"], w.at("cv", w.tick("cv") + 1))
                    w.tick("si")
                    act.activation(dst, tmp[:, :, :], ACT.Silu).then_inc(S["si"], 1)
                return job

            def cumulative_out(before):
                act.wait_ge(S["Tcst"], 1)
                act.activation(cs_t, tflat[0:HEADS, 0:TOK].rearrange("p (t l) -> p t l", t=NT), ACT.Copy)\
                    .then_inc(S["cst"], 1)
                act.wait_ge(S["cst"], 1)
                for t in range(NT):
                    act.dma_start(cs_dram[t].rearrange("(h l) -> h l", l=P), cs_t[:, t]).then_inc(S["cs_out"], 16)

            def decays(before=None):
                act.wait_ge(S["sg"], w.at("sg", w.tick("sg") + 1))
                w.tick("ex")
                act.activation(dec_all, dec_all, ACT.Exp, scale=-1.0).then_inc(S["ex"], 1)

            def cb_between(before=None):
                act.wait_ge(S["Tcb"], w.at("Tcb", w.tick("Tcb") + 1))
                w.tick("off")
                act.activation(cbo, tflat[:, P:2 * P], ACT.Copy).then_inc(S["off"], 1)

            def y_sums(before=None):
                act.wait_ge(S["yg"], w.at("yg", w.tick("yg") + 1))
                squares(lambda t: sq_sb[:, t], lambda t: ysum[:, t:t + 1], "ys")

            gate_z = take(lambda t: sz[:, t], "A", "sz", func=ACT.Silu, n=0)

            def conv_jobs(pair, taps, dst):
                return {3: [rows_out(pair)], 5: [conv_first(taps)], 7: [conv_silu(dst)]}

            static = taps_t[:, :, D_INNER // P:]
            unit({2: [take_narrow(dt_t, "A", 0)], 3: [rope_sines], 5: [softplus]})
            for n in range(4):
                if n == 1:
                    weights(None)
                jobs = conv_jobs("BA"[n % 2], static[:, :, 4 * n:4 * n + 4],
                                 bct[:, n // 2, 4 * (n % 2):4 * (n % 2) + 4])
                if n == 1:
                    jobs[4] = [cumulative_out]
                unit(jobs)
            unit(conv_jobs("B", gcv, xs_t))
            unit({3: [gate_z, decays], 4: [cb_between]})
            unit({0: [y_sums], 3: [rows_out("B", True)], 5: [act_hi(tiles(ya, 0))], 6: [conv_first(gcv)],
                  7: [conv_silu(xs_t)]})
            with w.rounds(GROUPS - 2, SSD_ROUND):
                unit({3: [gate_z], 6: [decays]})
                unit({0: [cb_between], 7: [y_sums]})
                unit({3: [act_hi(tiles(ya, 0))], 4: [rows_out("B", True)], 6: [conv_first(gcv)],
                      7: [conv_silu(xs_t)]})
            unit({3: [gate_z, decays], 4: [cb_between]})
            w.skip("hadd", 4)
            y_free = lambda before: act.wait_ge(S["used"], before)
            unit({0: [y_sums], 2: [y_free, act_hi(tiles(ya, 0))],
                  7: [sums(1, 0), act_hi(tiles(xa, 0))]})

            def mlp(layer, pp, first):
                n = 1 + 3 * layer
                src = tp[:, :, :]

                def middle(pair, j):
                    return {3: [take(lambda t: r_sb[:, t], pair, "r", ACT.Relu, n)],
                            5: [act_hi(tiles(ya, j), src, "Tu")]}

                unit(first)
                act.wait_ge(S["rs"], n + 1)
                with w.rounds(3, MLP_ROUND):
                    for j in range(4):
                        unit(middle(pp[j % 2], j))
                    for j in range(4):
                        unit()
                for j in range(4):
                    unit(middle(pp[j % 2], j))
                act.dma_start(p_sb, p[layer, 0].rearrange("(t p) n -> p t n", p=P)).then_inc(S["pin"], 16)
                for j in range(3):
                    jobs = {5: [sums(n + 1, j), act_hi(tiles(xa, j))]}
                    if j == 2:
                        jobs[0] = [act_hi(pt[0][:, :, :], tp[:, 0:2, :], "Tp")]
                    unit(jobs)

            def gates(layer, pp):
                n = 2 + 3 * layer

                def product(j):
                    return take(lambda t: prj[:, t, c512(512 * j)], pp[j % 2], "pj", late=j + 1)

                def gate(j):
                    take_gate = take(lambda t: r_sb[:, t], pp[j % 2], "gs", ACT.Sigmoid, n)

                    def job(before):
                        if layer and j:
                            act.wait_ge(S["hadd"], w.at("hadd", w.tick("hadd") + 1))
                        take_gate(before)
                    return job

                def own_before(job, back):
                    return lambda before: job(before - back)

                unit({3: [product(0)]}, halves=4)
                jobs = {m: [own_before(product(m + 1), 4)] for m in range(3)}
                jobs[3] = [sums(n, 3), act_hi(tiles(xa, 3))]
                unit(jobs)
                act.wait_ge(S["rs"], n + 1)
                for j in range(3):
                    jobs = {3: [gate(j)]}
                    if layer == 0:
                        jobs[6] = [sums(n + 1, j), act_hi(tiles(ya, j))]
                    unit(jobs)
                if layer == 0:
                    unit({3: [gate(3)], 6: [sums(n + 1, 3), act_hi(tiles(ya, 3))]})
                else:
                    gate(3)(w.k["G"])

            mlp(0, "BA", {1: [sums(1, 1), act_hi(tiles(xa, 1))], 3: [sums(1, 2), act_hi(tiles(xa, 2))],
                          5: [sums(1, 3), act_hi(tiles(xa, 3))]})
            gates(0, "BA")

            def take_c(dst, pair, col):
                def job(before):
                    act.wait_ge(S["rs"], 4)
                    if pair:
                        take(dst, pair, "ev", n=3)(before)
                        act.wait_ge(S["ev"], w.now("ev"))
                    else:
                        act.wait_ge(S["Tn"], 2)
                        for t in range(NT):
                            last = act.activation(dst(t), tbank[:, t * ROPE:(t + 1) * ROPE], ACT.Copy,
                                                  scale=rstd[:, 3, t:t + 1])
                        last.then_inc(S["kt"], 1)
                        act.wait_ge(S["kt"], 1)
                    squares(dst, lambda t: small[:, col + t:col + t + 1], "csq")
                return job

            def take_heads(start):
                jobs = (take(lambda t: qf[:, t, 0:512], "A", "ev", late=2),
                        take(lambda t: qf[:, t, 512:512 + Q2], "B", "ev", late=4),
                        take(lambda t: ktm[:, t], "A", "ev", late=6), take(lambda t: vtm[:, t], "B", "ev", late=8))
                qa, qb, keys, values = [lambda job=job: job(start) for job in jobs]

                def squared(job, dst, src):
                    def both():
                        job()
                        act.wait_ge(S["ev"], w.now("ev"))
                        w.tick("hs")
                        act.activation(dst, src, ACT.Square).then_inc(S["hs"], 1)
                    return both
                return qa, squared(qb, sqf, qf), squared(keys, ksq, ktm), values

            unit({0: [act_hi(tiles(xa, 0))], 2: [act_hi(tiles(xa, 1))],
                  3: [take_c(lambda t: r_sb[:, t], "B", 0)],
                  4: [act_hi(tiles(xa, 2))], 6: [act_hi(tiles(xa, 3))]})
            start = w.k["G"]
            split()
            act_hi(tiles(ya, 3))()
            split()
            take_c(lambda t: sq_sb[:, t], "A", 2)(start)
            take_narrow(krow_t, "B")(start)
            split()
            split(Q2)
            take_c(lambda t: kr_tm[:, t], None, 4)(start)
            split(Q2)
            qa, qb, keys, values = take_heads(start + 1)
            qa()
            act_hi(tiles(xa, 1))()
            def copied(dst, gain):
                act.wait_ge(S["Tq"], w.at("Tq", w.tick("Tq") + 1))
                w.tick("qt")
                act.activation(dst, tp[:, :, :], ACT.Copy, scale=gain).then_inc(S["qt"], 1)

            def exps(j):
                act.wait_ge(S["mx"], w.at("mx", w.tick("mx") + 1))
                b = STAT + 8 * (j % 2)
                act.activation(prob[j % 2][:, 0:P], mid[j % 2][:, 0:P], ACT.Exp, scale=SCALE,
                               bias=small[:, b + 2:b + 3], accum_out=small[:, b + 4:b + 5])
                w.tick("pe")
                act.activation(prob[j % 2][:, P:3 * P], mid[j % 2][:, P:3 * P], ACT.Exp, scale=SCALE,
                               bias=small[:, b + 3:b + 4], accum_out=small[:, b + 5:b + 6])\
                    .then_inc(S["pe"], 1)

            def prob_copy():
                act.wait_ge(S["Tpt"], w.at("Tpt", w.tick("Tpt") + 1))
                w.tick("ptc")
                act.activation(prob_t, tflat[:, 0:3 * P], ACT.Copy).then_inc(S["ptc"], 1)

            def attend(i, beside):
                def out_hi(j):
                    head = slice(i * QUAD + j, i * QUAD + j + 1) if isinstance(i, int) else \
                        bass.ds(i * QUAD + j, 1)
                    act_hi(ya[0][:, head], tflat[:, 512:512 + TOK], "To")()

                steps = (lambda: copied(q_t, vt[:, V_QN:V_QN + 1]), lambda: copied(qr_t, 1.0),
                         lambda: copied(k_t, vt[:, V_KN:V_KN + 1]),
                         lambda: exps(0), lambda: exps(1), prob_copy, lambda: out_hi(0),
                         prob_copy, lambda: exps(2), lambda: out_hi(1),
                         prob_copy, lambda: exps(3), lambda: out_hi(2), prob_copy, lambda: out_hi(3))
                for n, step in enumerate(steps):
                    for job in beside.get(n, ()):
                        job()
                    step()

            split()
            split()
            qb()
            split()
            split()
            keys()
            values()
            act.wait_ge(S["Tkr"], 1)
            act.activation(kr_t, tflat[:, 0:TOK], ACT.Copy).then_inc(S["krt"], 1)
            split()
            split()
            short_split = lambda: split(Q2)
            with w.rounds(QUADS - 1, QUAD_ROUND) as i:
                qa, qb, keys, values = take_heads(w.k["G"] - 2)
                attend(i, {2: [short_split], 3: [short_split, split, qa], 4: [split], 5: [qb, split],
                           6: [keys], 9: [split], 14: [split, split]})
                values()
            attend(QUADS - 1, {1: [split], 2: [split], 3: [split], 4: [split], 5: [split],
                               7: [split], 8: [split], 10: [split], 11: [split], 13: [split]})
            unit(halves=QUAD)
            unit({4: [sums(4, 0), act_hi(tiles(xa, 0))], 7: [sums(4, 1), act_hi(tiles(xa, 1))]})
            unit({5: [sums(4, 2), act_hi(tiles(xa, 2))]})
            mlp(1, "AB", {5: [sums(4, 3), act_hi(tiles(xa, 3))]})
            gates(1, "AB")

        @block.vector
        def _(dve):
            w = Walk(dve)

            def own(ins):
                ins.then_inc(S["dv"], 1)
                w.tick("dv")
                dve.wait_ge(S["dv"], w.now("dv"))

            def on(event, n=None):
                dve.wait_ge(S[event], w.at(event, w.tick(event) + 1))

            def signal(ins, event):
                w.tick(event)
                ins.then_inc(S[event], 1)

            def rest(cols=512):
                g = w.tick("G")
                dve.wait_ge(S["hi"], w.at("G", g + 1))
                dve.tensor_tensor(w_lo[:, g % SPL, :, 0:cols], raw[:, g % RAW, :, 0:cols],
                                  w_hi[:, g % SPL, :, 0:cols].bitcast(F32), ALU.subtract).then_inc(S["lo"], 1)

            def unit(jobs=None, halves=8, cols=512):
                before = w.k.get("G", 0)
                for n in range(halves):
                    rest(cols)
                    for job in (jobs or {}).get(n, ()):
                        job(before)

            def tiles(dst, blk):
                return dst[0][:, 4 * blk:4 * blk + 4], dst[1][:, 4 * blk:4 * blk + 4]

            def lo(dst, src=None):
                def job(before=None):
                    on("ahi")
                    signal(dve.tensor_tensor(dst[1], tmp[:, :, :] if src is None else src,
                                             dst[0].bitcast(F32), ALU.subtract), "act")
                return job

            def gain(col, event="Th"):
                def job(before=None):
                    on(event)
                    g = gng if col is None else vt[:, col:col + 4]
                    signal(dve.tensor_tensor(tmp[:, :, :], tp[:, :, :],
                                             g.unsqueeze(2).to_broadcast([P, 4, TOK]), ALU.mult), "tm")
                return job

            def add(pair, blk, late=0):
                def job(before):
                    dve.wait_ge(S["used"], w.at("G", before + late))
                    for t in range(NT):
                        v = h[:, t, c512(512 * blk)]
                        last = dve.tensor_tensor(v, acc[pair][t][:, :], v, ALU.add)
                    signal(last, "hadd")
                return job

            on("Tv")
            for n, cols in enumerate(V_ROWS):
                last = dve.tensor_copy(vt[:, P * n:P * n + cols], bank[0][:, P * n:P * n + cols])
            last.then_inc(S["vt"], 1)
            dve.wait_ge(S["vt"], 1)

            def first_gain(blk):
                on("Th")
                if blk == NB - 1:
                    dve.wait_ge(S["act"], 1)
                for m, psum in enumerate(first_psum[blk]):
                    g = vt[:, V_MIX + 4 * blk + 2 * m:V_MIX + 4 * blk + 2 * m + 2]
                    last = dve.tensor_tensor(first_tmp[blk][:, 2 * m:2 * m + 2], psum,
                                             g.unsqueeze(2).to_broadcast([P, 2, TOK]), ALU.mult)
                signal(last, "tm")

            def first_lo(blk):
                lo(tiles(xa, blk), first_tmp[blk])()

            for step, blk in ((first_gain, 0), (first_gain, 1), (first_gain, 2), (first_lo, 0), (first_gain, 3),
                              (first_lo, 1), (first_lo, 2), (first_lo, 3)):
                step(blk)
            rest()

            def rope_angles(before):
                dve.wait_ge(S["loads"], 16 * 6)
                dve.wait_ge(S["setup"], 2)
                own(dve.tensor_copy(pos_f, pos_i[:, :]))
                for t in range(NT):
                    last = dve.tensor_scalar(ang[:, t], freq, pos_f[:, t:t + 1], None, ALU.mult)
                own(last)
                magic = 1.5 * 2.0 ** 23
                own(dve.tensor_scalar(turns, ang, 1.0 / (2 * math.pi), magic, ALU.mult, ALU.add))
                own(dve.tensor_scalar(turns, turns, magic, None, ALU.subtract))
                rest_of = 2 * math.pi
                for bits in (5, 14, 23, 34):
                    c = round(rest_of * 2 ** bits) / 2 ** bits
                    rest_of -= c
                    own(dve.scalar_tensor_tensor(ang, turns, -c, ang, ALU.mult, ALU.add))
                own(dve.tensor_scalar(ang, ang, PI_IN, -PI_IN, ALU.min, ALU.max))
                own(dve.scalar_tensor_tensor(turns, ang, -1.0, ang, ALU.mult, ALU.max))
                dve.tensor_scalar(turns, turns, -1.0, math.pi / 2, ALU.mult, ALU.add).then_inc(S["rope_arg"], 1)

            def dt_row(before):
                dve.wait_ge(S["rs"], 1)
                dve.wait_ge(S["Tn"], 1)
                for t in range(NT):
                    last = dve.scalar_tensor_tensor(pad[0][:, t], tbank[:, t * HEADS:(t + 1) * HEADS],
                                                    rstd[:, 0, t:t + 1],
                                                    bc[:, 0], ALU.mult, ALU.add)
                own(last)
                dve.scalar_tensor_tensor(pad[1], pad[0], -1.0, pad[0], ALU.mult, ALU.min).then_inc(S["dt_x"], 1)

            def dt_log(before):
                dve.wait_ge(S["dt_e"], 1)
                own(dve.tensor_scalar(pad[2], pad[1], 1.0, None, ALU.add))
                dve.tensor_scalar(hq[:, WGT:WGT + 2], pad[2], -1.0, TINY, ALU.add, ALU.add).then_inc(S["dt_u"], 1)
                dve.wait_ge(S["dt_u"], 1)
                own(dve.reciprocal(hq[:, WGT:WGT + 2], hq[:, WGT:WGT + 2]))
                own(dve.tensor_tensor(pad[1], pad[1], hq[:, WGT:WGT + 2], ALU.mult))
                dve.wait_ge(S["dt_ln"], 1)
                own(dve.scalar_tensor_tensor(pad[1], pad[3], TINY, pad[1], ALU.add, ALU.mult))
                own(dve.scalar_tensor_tensor(hq[:, DT:DT + 2], pad[0], 0.0, pad[1], ALU.max, ALU.add))
                dve.scalar_tensor_tensor(hq[:, DA:DA + 2], hq[:, DT:DT + 2], -1.0,
                                         bc[:, 1].unsqueeze(1).to_broadcast([P, NT, HEADS]),
                                         ALU.mult, ALU.mult).then_inc(S["dt_a"], 1)

            def dt_sums(before):
                dve.wait_ge(S["Tcs"], 1)
                cs = tbank[:, 0:NT * HEADS].rearrange("p (t n) -> p t n", t=NT)
                for t in range(NT):
                    dve.tensor_copy(hq[:, SKIP + t], bc[:, 2])
                own(dve.tensor_scalar(hq[:, NCS:NCS + 2], cs, -1.0, None, ALU.mult))
                dve.tensor_tensor(pad[0][:, 0], tbank[:, 2 * HEADS:3 * HEADS], hq[:, NCS], ALU.add)
                dve.tensor_copy(pad[0][:, 1], cs[:, 1]).then_inc(S["dt_w"], 1)

            def conv_taps(taps, lags):
                def job(before=None):
                    if lags[0] == 1:
                        on("c0")
                    for d in lags:
                        for j in range(4):
                            v = tmp[:, j, d:TOK]
                            last = dve.scalar_tensor_tensor(v, tp[:, j, 0:TOK - d],
                                                            taps[:, CONV_W - 1 - d, j:j + 1], v,
                                                            ALU.mult, ALU.add)
                        if d < lags[-1]:
                            own(last)
                    if lags[-1] == CONV_W - 1:
                        signal(last, "cv")
                    else:
                        own(last)
                return job

            def heads(v, kind):
                return hqg[:, kind].unsqueeze(2).to_broadcast([P, GH, HDIM])

            def parameters(before=None):
                on("gp")

            def exponents(before=None):
                dve.wait_ge(S["csb"], w.at("csb", w.tick("csb")) * (16 * NT) + 16 * NT)
                for b in range(NT):
                    for n in range(GH):
                        last = dve.tensor_scalar(dec[b][:, n], dec[b][:, n], hqg[:, NCS + b, n:n + 1], 0.0,
                                                 ALU.subtract, ALU.max)
                signal(last, "sg")

            def x_dt(before=None):
                on("Tb")
                for t in range(NT):
                    v = ttok[:, t].rearrange("p (h d) -> p h d", h=GH)
                    last = dve.tensor_tensor(xdt[:, t], v, heads(v, DT + t), ALU.mult)
                    dve.tensor_tensor(y4[:, t], v, heads(v, SKIP + t), ALU.mult)
                own(last)
                signal(dve.tensor_tensor(xw, xdt[:, 0], heads(xw, WGT), ALU.mult), "xd")

            def decay_cb(before=None):
                on("off")
                for b in range(NT):
                    last = dve.tensor_tensor(cbd[:, b], tflat[:, 2 * P * b:2 * P * b + P], upper[:, :], ALU.mult)
                own(last)
                on("ex")
                for b in range(NT):
                    v = cbd[:, b].unsqueeze(1).to_broadcast([P, GH, P])
                    last = dve.tensor_tensor(dec[b], v, dec[b], ALU.mult)
                signal(last, "mm")

            def y_gate(before=None):
                on("Ty")
                dve.tensor_tensor(carried, tbank.rearrange("p (h d) -> p h d", h=GH),
                                  heads(carried, WGT + 1), ALU.mult)
                for t in range(NT):
                    last = dve.tensor_tensor(sq_sb[:, t], mid[t][:, :], sq_sb[:, t], ALU.add)
                own(last)
                own(dve.tensor_tensor(y4[:, 1], y4[:, 1], carried, ALU.add))
                on("sz")
                signal(dve.tensor_tensor(sq_sb[:, :, :], sq_sb[:, :, :], sz, ALU.mult), "yg")

            def y_norm(before=None):
                on("yr")
                for t in range(NT):
                    last = dve.tensor_scalar(sq_sb[:, t], sq_sb[:, t], yroot[:, t:t + 1], None, ALU.mult)
                signal(last, "yn")

            def y_gain(before=None):
                gain(None, "Tyt")()

            def y_lo(before=None):
                lo(tiles(ya, 0))()

            def before_out(job):
                return lambda before: job(before - 8)

            static = taps_t[:, :, D_INNER // P:]
            unit({0: [rope_angles], 3: [dt_row], 5: [dt_log]})
            for n in range(4):
                jobs = {6: [conv_taps(static[:, :, 4 * n:4 * n + 4], (1, 2, 3))]}
                if n == 0:
                    jobs[2] = [dt_sums]
                unit(jobs)
            unit({6: [conv_taps(gcv, (1, 2, 3))]})
            unit({0: [parameters, exponents], 3: [x_dt], 6: [decay_cb]})
            unit({0: [y_gate], 2: [y_norm], 5: [y_gain, y_lo], 7: [conv_taps(gcv, (1, 2, 3))]})
            with w.rounds(GROUPS - 2, SSD_ROUND):
                unit({2: [parameters, exponents], 5: [add("B", 0, 2)], 6: [x_dt], 7: [add("A", 1, 4)]})
                unit({1: [before_out(add("B", 2, 6))], 2: [decay_cb],
                      3: [before_out(add("A", 3, 8))], 5: [y_gate]})
                unit({0: [y_norm], 2: [y_gain], 3: [y_lo], 7: [conv_taps(gcv, (1, 2, 3))]})
            unit({0: [parameters, x_dt], 1: [exponents], 4: [decay_cb], 5: [add("B", 0, 2)],
                  7: [add("A", 1, 4), y_gate]})
            unit({0: [y_norm], 1: [before_out(add("B", 2, 6))],
                  2: [y_gain, y_lo, before_out(add("A", 3, 8))],
                  5: [add("B", 0, 2)], 7: [gain(V_MLP), add("A", 1, 4)]})

            def mlp(layer, pp, first):
                def middle(pair, j):
                    def square(before):
                        on("r")
                        signal(dve.tensor_tensor(sq_sb[:, :, :], r_sb[:, :, :], r_sb[:, :, :], ALU.mult), "sq")
                    return {3: [square], 5: [lo(tiles(ya, j), tp[:, :, :])]}

                unit(first)
                with w.rounds(3, MLP_ROUND):
                    for j in range(4):
                        unit(middle(pp[j % 2], j))
                    for j in range(4):
                        unit({3: [add(pp[j % 2], j)]})
                for j in range(4):
                    unit(middle(pp[j % 2], j))
                for j in range(3):
                    jobs = {3: [add(pp[j % 2], j)], 5: [gain(V_PLE + 16 * layer + 4 * j)], 6: [lo(tiles(xa, j))]}
                    if j == 2:
                        jobs[0] = [lo((pt[0][:, :, :], pt[1][:, :, :]), tp[:, 0:2, :])]
                    unit(jobs)

            def gates(layer, pp):
                def gated(j):
                    def job(before):
                        on("gs")
                        if j == 0:
                            dve.wait_ge(S["pj"], 4 * layer + 4)
                        own(dve.tensor_tensor(r_sb[:, :, :], r_sb[:, :, :], prj[:, :, c512(512 * j)], ALU.mult))
                        v = h[:, :, c512(512 * j)]
                        signal(dve.tensor_tensor(v, v, r_sb[:, :, :], ALU.add), "hadd")
                    return job

                unit({3: [add(pp[1], 3)]}, halves=4)
                unit({1: [gain(V_PLE + 16 * layer + 12)], 4: [lo(tiles(xa, 3))]})
                for j in range(3):
                    jobs = {3: [gated(j)]}
                    if layer == 0:
                        jobs[6] = [gain(V_MIX + 16 + 4 * j)]
                        jobs[7] = [lo(tiles(ya, j))]
                    unit(jobs)
                if layer == 0:
                    unit({3: [gated(3)], 6: [gain(V_MIX + 16 + 12)], 7: [lo(tiles(ya, 3))]})
                else:
                    gated(3)(None)

            add_out = lambda n: before_out(add("BA"[n % 2], n, 2 * n + 2))
            mlp(0, "BA", {0: [lo(tiles(xa, 0))], 1: [gain(V_MLP + 4), add_out(2)], 2: [lo(tiles(xa, 1))],
                          3: [gain(V_MLP + 8), add_out(3)], 4: [lo(tiles(xa, 2))],
                          5: [gain(V_MLP + 12)], 6: [lo(tiles(xa, 3))]})
            gates(0, "BA")
            kv = lambda j: gain(V_KVIN + 4 * j)

            def normalised(v, col, n):
                dve.wait_ge(S["crs"], n)
                for t in range(NT):
                    last = dve.tensor_scalar(v[:, t], v[:, t], small[:, col + t:col + t + 1], None, ALU.mult)
                return last

            def normal_cq(before):
                normalised(r_sb, 6, 1).then_inc(S["cn"], 1)

            jobs = {n: [kv(n // 2) if n % 2 == 0 else lo(tiles(xa, n // 2))] for n in range(8)}
            jobs[7].append(normal_cq)
            unit(jobs)
            dve.memset(krp, 0.0)
            own(dve.memset(qrp, 0.0))
            rest()
            gain(V_CQ)()
            lo(tiles(ya, 3))()
            rest()
            rest()
            rest(Q2)
            normalised(sq_sb, 8, 2).then_inc(S["cn"], 1)
            rest(Q2)
            gain(V_CKV)()
            lo(tiles(xa, 1))()
            dve.wait_ge(S["rope"], 1)

            def rotate(dst, v, cs, sn, a, b):
                dve.tensor_tensor(a, v[0], cs, ALU.mult)
                own(dve.tensor_tensor(b, v[1], sn, ALU.mult))
                own(dve.tensor_tensor(dst[0], a, b, ALU.subtract))
                dve.tensor_tensor(a, v[1], cs, ALU.mult)
                own(dve.tensor_tensor(b, v[0], sn, ALU.mult))
                return dve.tensor_tensor(dst[1], a, b, ALU.add)

            qn = q8[:, :, 0:NOPE]
            k8 = ktm.rearrange("p t n -> p (t n)").rearrange("p (n d) -> p n d", d=NOPE)

            def q_sums():
                on("hs")
                dve.tensor_reduce(small[:, 32:40], sq8[:, :, NOPE:QH], AX.X, ALU.add)
                signal(dve.tensor_reduce(small[:, 16:24], sq8[:, :, 0:NOPE], AX.X, ALU.add), "st")

            def q_scaled():
                on("qrs")
                signal(dve.tensor_tensor(qn, qn, small[:, 48:56].unsqueeze(2).to_broadcast([P, NH, NOPE]),
                                         ALU.mult), "qn")

            def k_sums():
                on("hs")
                signal(dve.tensor_reduce(small[:, 24:32].rearrange("p (t n) -> p t n", t=NT),
                                         ksq.rearrange("p t (n d) -> p t n d", d=NOPE), AX.X, ALU.add), "st")

            def k_scaled():
                on("qrs")
                signal(dve.tensor_tensor(k8, k8, small[:, 56:64].unsqueeze(2).to_broadcast([P, NH, NOPE]),
                                         ALU.mult), "kn")

            def attend(i, beside):
                def maxima(j):
                    on("sc")
                    b = STAT + 8 * (j % 2)
                    dve.tensor_reduce(small[:, b:b + 1], mid[j % 2][:, 0:P], AX.X, ALU.max)
                    own(dve.tensor_reduce(small[:, b + 1:b + 2], mid[j % 2][:, P:3 * P], AX.X, ALU.max))
                    signal(dve.tensor_scalar(small[:, b + 2:b + 4], small[:, b:b + 2], -SCALE, None, ALU.mult), "mx")

                def probabilities(j):
                    on("pe")
                    b = STAT + 8 * (j % 2)
                    own(dve.reciprocal(small[:, b + 6:b + 8], small[:, b + 4:b + 6]))
                    v = prob[j % 2]
                    dve.tensor_scalar(v[:, 0:P], v[:, 0:P], small[:, b + 6:b + 7], None, ALU.mult)
                    signal(dve.tensor_scalar(v[:, P:3 * P], v[:, P:3 * P], small[:, b + 7:b + 8], None, ALU.mult), "pn")

                def out_lo(j):
                    head = slice(i * QUAD + j, i * QUAD + j + 1) if isinstance(i, int) else \
                        bass.ds(i * QUAD + j, 1)
                    lo((ya[0][:, head], ya[1][:, head]), tflat[:, 512:512 + TOK].unsqueeze(1))()

                steps = ((maxima, 0), (maxima, 1), (probabilities, 0), (probabilities, 1), (out_lo, 0), (maxima, 2),
                         (probabilities, 2), (out_lo, 1), (maxima, 3), (probabilities, 3), (out_lo, 2), (out_lo, 3))
                for n, (step, j) in enumerate(steps):
                    for job in beside.get(n, ()):
                        job()
                    step(j)

            rest()
            rest()
            q_sums()
            own(normalised(kr_tm, 10, 3))
            own(dve.tensor_tensor(kr_tm, kr_tm, bc[:, 4].unsqueeze(1).to_broadcast([P, NT, ROPE]), ALU.mult))
            two = lambda v: (v[:, :, 0:HALF], v[:, :, HALF:ROPE])
            pad_a, pad_b = prob[0][:, 0:NT * HALF], prob[0][:, NT * HALF:2 * NT * HALF]
            pad_a, pad_b = (v.rearrange("p (a b) -> p a b", a=NT) for v in (pad_a, pad_b))
            rotate(two(krp), two(kr_tm), cos[:, :, :], sin[:, :, :], pad_a, pad_b).then_inc(S["cn"], 1)
            rest()
            rest()
            k_sums()
            q_scaled()
            rest()
            k_scaled()
            rest()
            short_rest = lambda: rest(Q2)
            with w.rounds(QUADS - 1, QUAD_ROUND) as i:
                attend(i, {0: [short_rest, short_rest, rest], 1: [rest], 3: [rest], 6: [q_sums], 7: [k_sums, rest],
                           10: [q_scaled], 11: [k_scaled]})
                rest()
                rest()
            attend(QUADS - 1, {0: [rest, rest, rest], 1: [rest], 3: [rest], 4: [rest], 6: [rest],
                               8: [rest], 9: [rest], 11: [rest]})
            unit({3: [add("A", 0, 2)]}, halves=QUAD)
            unit({1: [add("B", 1)], 4: [gain(V_MLP + 16)], 5: [lo(tiles(xa, 0))],
                  7: [gain(V_MLP + 20), lo(tiles(xa, 1))]})
            unit({3: [add("A", 2)], 5: [gain(V_MLP + 24)], 6: [lo(tiles(xa, 2))]})
            mlp(1, "AB", {3: [add("B", 3)], 5: [gain(V_MLP + 28)], 6: [lo(tiles(xa, 3))]})
            gates(1, "AB")

        @block.tensor
        def _(pe):
            w = Walk(pe)

            def hold(banks, event):
                for b in banks:
                    if b in w.busy:
                        name, k = w.busy[b]
                        pe.wait_ge(S[name], w.at(name, k))
                k = w.tick(event) + 1
                for b in banks:
                    w.busy[b] = event, k

            def on(event):
                pe.wait_ge(S[event], w.at(event + "'", w.tick(event + "'") + 1))

            def half_chunk(x, tile, pair, first, last, cols=512):
                g = w.tick("G")
                pe.wait_ge(S["lo"], w.at("G", g + 1))
                for k in range(2):
                    for t in range(NT):
                        rows = slice(t * P, t * P + P)
                        dst = acc[pair][t][:, 0:cols]
                        xh, xl = x[0][:, tile + k, rows], x[1][:, tile + k, rows]
                        wh, wl = w_hi[:, g % SPL, k, 0:cols], w_lo[:, g % SPL, k, 0:cols]
                        pe.matmul(dst, xh, wh, start=first and k == 0, stop=False)
                        pe.matmul(dst, xh, wl, start=False, stop=False)
                        mm = pe.matmul(dst, xl, wh, start=False, stop=last and k == 1)
                    if k == 1:
                        mm.then_inc(S["used"], 1)
                    yield

            def chunk(*args):
                for _ in half_chunk(*args):
                    pass

            def narrow_chunk(x, pair, need=0):
                hold(pair, "nt")
                g = w.tick("G")
                pe.wait_ge(S["lo"], g + 1)
                hi, lo_ = narrow(w_hi[:, g % SPL]), narrow(w_lo[:, g % SPL])
                dst = acc[pair][0][0:HEADS, 0:TOK]
                for k in range(KT):
                    if need and k % 4 == 0:
                        pe.wait_ge(S["act"], need + k // 4)
                    pe.matmul(dst, hi[:, k], x[0][:, k], start=k == 0, stop=False)
                    pe.matmul(dst, lo_[:, k], x[0][:, k], start=False, stop=False)
                    mm = pe.matmul(dst, hi[:, k], x[1][:, k], start=False, stop=k == KT - 1)
                mm.then_inc(S["used"], 1)

            def turn_narrow(src, event):
                on("nt")
                hold("T", event)
                for t in range(NT):
                    last = pe.transpose(tbank[:, t * HEADS:(t + 1) * HEADS], src[:, t * P:t * P + P],
                                        ident[0:HEADS, 0:HEADS])
                last.then_inc(S["Tn"], 1)

            def unit(x, pair, event, jobs=None, need=None):
                hold(pair, event)
                for n in range(8):
                    if need and n % 2 == 0:
                        pe.wait_ge(S["act"], w.at("act", need[n // 2]))
                    chunk(x, 2 * n, pair, n == 0, n == 7)
                    for job in (jobs or {}).get(n, ()):
                        job()

            def flip(src, per, n, m):
                for j in range(n):
                    for t in range(m):
                        last = pe.transpose(per(j, t), src(j, t), ident[:, :])
                return last

            def feature(j, t):
                return tp[:, j, t * P:t * P + P]

            def turn_h(blk, updates):
                def job():
                    if updates:
                        pe.wait_ge(S["hadd"], updates)
                    hold("T", "act")
                    flip(lambda j, t: h[:, t, 512 * blk + P * j:512 * blk + P * j + P], feature, 4, NT)\
                        .then_inc(S["Th"], 1)
                return job

            pe.wait_ge(S["setup"], 1)
            pe.wait_ge(S["xin"], 16 * NT)
            for blk in range(NB):
                if blk == 0:
                    hold("T", "act")
                else:
                    w.skip("act")
                src = lambda j, t: h[:, t, 512 * blk + P * j:512 * blk + P * j + P]
                dst = lambda j, t: first_psum[blk][j // 2][:, j % 2, t * P:t * P + P]
                if blk == NB - 1:
                    pe.wait_ge(S["vt"], 1)
                flip(src, dst, 4, NT).then_inc(S["Th"], 1)
                if blk == 0:
                    pe.wait_ge(S["vec"], 16 * 12)
                    for n, cols in enumerate(V_ROWS):
                        last = pe.transpose(bank[0][:, n * P:n * P + cols], vrows[0:cols, n], ident[0:cols, 0:cols])
                    last.then_inc(S["Tv"], 1)
            narrow_chunk(xa, "A", 1)

            def cumulative():
                pe.wait_ge(S["dt_a"], 1)
                hold("T", "dt_w")
                for t in range(NT):
                    pe.matmul(tbank[:, t * HEADS:(t + 1) * HEADS], upper[:, :], hq[:, DA + t], start=True, stop=True)
                pe.matmul(tbank[:, NT * HEADS:(NT + 1) * HEADS], upper[:, P - 1:P].to_broadcast([P, P]),
                          hq[:, DA], start=True, stop=True).then_inc(S["Tcs"], 1)

            def turn_rows():
                on("xr")
                hold("T", "cv")
                flip(lambda j, t: r_sb[:, t, P * j:P * j + P], feature, 4, NT).then_inc(S["Tc"], 1)

            def turn_back():
                on("si")
                hold("T", "xd")
                flip(lambda j, t: xs_t[:, j, t * P:t * P + P], lambda j, t: ttok[:, t, P * j:P * j + P], 4, NT)\
                    .then_inc(S["Tb"], 1)

            def turn_cumulative():
                pe.wait_ge(S["dt_w"], 1)
                hold("T", "cst")
                for t in range(NT):
                    last = pe.transpose(tflat[0:HEADS, t * P:(t + 1) * P], hq[:, NCS + t], ident[:, :])
                last.then_inc(S["Tcst"], 1)

            def c_b():
                hold("T", "mm")
                pe.matmul(tflat[:, 0:TOK], bg[:, 0, 0:P], bg[:, 1, :], start=True, stop=True)
                pe.matmul(tflat[:, TOK:TOK + P], bg[:, 0, P:TOK], bg[:, 1, P:TOK], start=True, stop=True)\
                    .then_inc(S["Tcb"], 1)

            def y_products():
                hold(("T", "M"), "yg")
                for b in range(NT):
                    for n in range(GH):
                        pe.matmul(mid[b][:, HDIM * n:HDIM * n + HDIM], dec[b][:, n], xdt[:, b, n],
                                  start=True, stop=True)
                pe.matmul(tbank, cbo, xw.rearrange("p h d -> p (h d)"), start=True, stop=True)\
                    .then_inc(S["Ty"], 1)

            def turn_y():
                on("yn")
                hold("T", "act")
                flip(lambda j, t: sq_sb[:, t, P * j:P * j + P], feature, 4, NT).then_inc(S["Tyt"], 1)

            def out_piece(jobs, pairs):
                pe.wait_ge(S["act"], w.now("act"))
                for n in range(NB):
                    hold(pairs[n % 2], "hadd")
                    for k in range(2):
                        chunk(ya, 2 * k, pairs[n % 2], k == 0, k == 1)
                        for job in jobs.get(2 * n + k, ()):
                            job()

            pe.wait_ge(S["setup"], 2)
            unit(xa, "B", "xr", {1: [lambda: turn_narrow(dt_t, "dt_x")]})
            for n in range(3):
                jobs = {1: [turn_rows]}
                if n < 2:
                    jobs[0] = [(cumulative, turn_cumulative)[n]]
                unit(xa, "AB"[n % 2], "xr", jobs)
            unit(xa, "B", "xr", {1: [turn_rows]})
            w.skip("si'", 4)
            unit(xa, "A", "sz", {1: [turn_rows]})
            unit(xa, "B", "xr", {0: [turn_back], 1: [c_b], 4: [y_products]})
            unit(xa, "A", "sz", {1: [turn_y], 3: [turn_rows]})
            with w.rounds(GROUPS - 2, SSD_ROUND):
                out_piece({1: [turn_back], 4: [c_b]}, "BA")
                unit(xa, "B", "xr", {0: [y_products], 6: [turn_y]})
                unit(xa, "A", "sz", {2: [turn_rows]})
            turn_back()
            out_piece({1: [c_b], 3: [y_products], 6: [turn_y]}, "BA")
            out_piece({3: [turn_h(0, 29)], 6: [turn_h(1, 30)]}, "BA")

            def needs(posted):
                return [w.k["act"] - posted + 1 + n for n in range(4)]

            def mlp(layer, pp, turns, posted):
                def turn_middle():
                    on("sq")
                    hold("T", "act")
                    flip(lambda j, t: sq_sb[:, t, P * j:P * j + P], feature, 4, NT).then_inc(S["Tu"], 1)

                def turn_p():
                    pe.wait_ge(S["pin"], 16 * (layer + 1))
                    hold("T", "act")
                    flip(lambda j, t: p_sb[:, t, P * j:P * j + P], feature, 2, NT).then_inc(S["Tp"], 1)

                base = 32 + 24 * layer + 12
                unit(xa, pp[0], "r", turns, needs(posted))
                with w.rounds(3, MLP_ROUND):
                    for j in range(1, 4):
                        unit(xa, pp[j % 2], "r", {1: [turn_middle]})
                    unit(ya, pp[0], "hadd", {1: [turn_middle]}, needs(3))
                    for j in range(1, 4):
                        unit(ya, pp[j % 2], "hadd")
                    unit(xa, pp[0], "r")
                for j in range(1, 4):
                    unit(xa, pp[j % 2], "r", {1: [turn_middle]})
                unit(ya, pp[0], "hadd", {1: [turn_middle]}, needs(3))
                unit(ya, pp[1], "hadd", {1: [turn_h(0, base + 1)]})
                unit(ya, pp[0], "hadd", {1: [turn_h(1, base + 2)], 4: [turn_p]})
                unit(ya, pp[1], "hadd", {1: [turn_h(2, base + 3)]})
                c = w.k["act"]
                pe.wait_ge(S["act"], c - 1)
                for n in range(NB):
                    hold(pp[n % 2], "pj")
                    chunk(pt, 0, pp[n % 2], True, True)
                    if n == 1:
                        turn_h(3, base + 4)()
                jobs = lambda n, slot: {slot: [turn_h(n, base + 5 + n)]} if layer == 0 else {}
                unit(xa, pp[0], "gs", None, [c - 3, c - 2, c, c + 1])
                for n in range(3):
                    unit(xa, pp[(n + 1) % 2], "gs", jobs(n, 3))
                w.skip("hadd", NB)
                return base

            base = mlp(0, "BA", {0: [turn_h(2, 31)], 2: [turn_h(3, 32)]}, 2)
            unit(ya, "B", "ev", {3: [turn_h(3, base + 8)], 5: [turn_h(0, 0)], 7: [turn_h(1, 0)]}, needs(3))

            def turn_c(n):
                def job():
                    src = (r_sb, sq_sb)[n]
                    pe.wait_ge(S["cn"], n + 1)
                    hold("T", "act")
                    flip(lambda j, t: src[:, t, P * j:P * j + P], feature, 4, NT).then_inc(S["Th"], 1)
                return job

            unit(xa, "A", "ev", {1: [turn_h(2, 0)], 3: [turn_h(3, 0)], 6: [turn_c(0)]}, needs(2))
            narrow_chunk(xa, "B")
            pe.wait_ge(S["act"], w.k["act"])

            def heads(jobs=None):
                for n, (x, pair, tile, cols) in enumerate(((ya, "A", 12, 512), (ya, "B", 12, Q2),
                                                           (xa, "A", 4, 512), (xa, "B", 4, 512))):
                    for k in range(2):
                        if k == 0:
                            hold(pair, "ev")
                        yield from half_chunk(x, tile + 2 * k, pair, k == 0, k == 1, cols)

            def fill(chunks, n=1):
                for _ in range(n):
                    next(chunks)

            chunks = heads()
            fill(chunks, 2)
            turn_narrow(krow_t, "kt")
            fill(chunks, 2)
            turn_c(1)()
            c_kv = w.k["act"]
            fill(chunks, 4)
            pe.wait_ge(S["act"], c_kv)
            fill(chunks, 8)
            pe.wait_ge(S["cn"], 3)
            hold("T", "krt")
            flip(lambda j, t: krp[:, t], lambda j, t: tflat[:, t * P:t * P + P], 1, NT).then_inc(S["Tkr"], 1)
            pe.wait_ge(S["krt"], 1)

            def attend(chunks, plan):
                plan, taken_out = iter(plan), w.k["ev"]

                def beside():
                    fill(chunks, next(plan))

                k4 = ktm.rearrange("p t (n d) -> p t n d", d=NOPE)
                q4 = qf.rearrange("p t (n d) -> p t n d", d=QH)
                r4 = qrp.rearrange("p (t n) d -> p t n d", t=NT)
                for src, event in ((q4[:, :, :, 0:NOPE], "qn"), (r4, "qrot"), (k4, "kn")):
                    on(event)
                    hold("TU", "qt")
                    flip(lambda j, t: src[:, t, j], feature, QUAD, NT).then_inc(S["Tq"], 1)
                    beside()

                def scores(j):
                    if j >= 2:
                        pe.wait_ge(S["pe"], w.now("pe", 1 - j))
                    if j == 0:
                        pe.wait_ge(S["qt"], w.now("qt"))
                    m = mid[j % 2]
                    pe.matmul(m[:, 0:3 * P], identb[:, :], amask[:, :], start=True, stop=False)
                    for t, (a, b) in enumerate(((0, P), (P, 3 * P))):
                        rows = slice(t * P, t * P + P)
                        pe.matmul(m[:, a:b], q_t[:, j, rows], k_t[:, j, 0:b - a], start=False, stop=False)
                        last = pe.matmul(m[:, a:b], qr_t[:, j, rows], kr_t[:, 0:b - a], start=False, stop=t == 1)
                    last.then_inc(S["sc"], 1)

                def turn_probabilities(j):
                    on("pn")
                    hold("T", "ptc")
                    for n in range(3):
                        last = pe.transpose(tflat[:, n * P:n * P + P], prob[j % 2][:, n * P:n * P + P], ident[:, :])
                    last.then_inc(S["Tpt"], 1)

                def weigh(j):
                    if j == 0:
                        pe.wait_ge(S["ev"], w.at("ev", taken_out))
                    pe.wait_ge(S["ptc"], w.now("ptc"))
                    hold("U", "act")
                    v = [vtm[:, t, j * VH:(j + 1) * VH] for t in range(NT)]
                    o = tflat[:, 512:512 + TOK]
                    pe.matmul(o, v[0], prob_t[:, 0:TOK], start=True, stop=False)
                    pe.matmul(o[:, P:TOK], v[1], prob_t[:, TOK:3 * P], start=False, stop=True)\
                        .then_inc(S["To"], 1)

                scores(0)
                beside()
                scores(1)
                beside()
                for j in range(QUAD):
                    turn_probabilities(j)
                    beside()
                    weigh(j)
                    if j + 2 < QUAD:
                        scores(j + 2)
                beside()
                w.skip("pe", 4)
                w.busy["T"] = w.busy["U"]

            w.busy["T"] = w.busy["U"] = "act", w.k["act"]
            with w.rounds(QUADS - 1, QUAD_ROUND):
                attend(heads(), (2, 2, 2, 2, 2, 2, 1, 1, 1, 1))

            def out_rows(tiles):
                for pair in "AB":
                    if tiles[0] == 0:
                        hold(pair, "hadd")
                    for k in tiles:
                        yield from half_chunk(ya, k, pair, k == 0, k == KT - 2)

            attend(out_rows(range(0, KT - QUAD, 2)), (2, 2, 2, 2, 2, 2, 2, 2, 2, 6))
            pe.wait_ge(S["act"], w.k["act"])
            fill(out_rows(range(KT - QUAD, KT, 2)), 2 * QUAD)
            unit(ya, "A", "hadd", {2: [turn_h(0, 53)], 5: [turn_h(1, 54)]})
            unit(ya, "B", "hadd", {1: [turn_h(2, 55)]})
            mlp(1, "AB", {1: [turn_h(3, 56)]}, 3)


_INS = ["x", "p", "positions", "ln_mix", "ln_mlp", "mlp_w1", "mlp_w2", "ple_norm", "ple_gate_w", "ple_proj_w",
        "ssm_in_w", "ssm_conv_w", "ssm_conv_b", "ssm_dt_bias", "ssm_a_log", "ssm_d", "ssm_norm", "ssm_out_w",
        "kv_in_norm", "w_dkv", "ckv_norm", "w_kr", "w_uk", "w_uv", "k_nope_norm", "k_rope_norm",
        "w_dq", "cq_norm", "w_uq", "q_nope_norm", "q_rope_norm", "mla_out_w"]


def kernel(**inputs):
    import concourse.bacc as _bacc
    from concourse.bass_utils import run_bass_kernel_spmd as _run

    nc = _bacc.Bacc("TRN2", target_bir_lowering=False, num_devices=1)
    arrays, args = {}, []
    for name in _INS:
        a = np.ascontiguousarray(inputs[name])
        arrays[f"in_{name}"] = a
        args.append(nc.dram_tensor(f"in_{name}", a.shape, mybir.dt.from_np(a.dtype), kind="ExternalInput").ap())
    out = nc.dram_tensor("out_0", (1, TOK, D), F32, kind="ExternalOutput").ap()
    trunk_kernel(nc, *args, out)
    r = _run(nc, [arrays], core_ids=[0])
    return r.results[0]["out_0"]
```
